# Optimizing a Trainium2 kernel written in Bass

```python
import jax
import jax.numpy as jnp
from jax import lax
import numpy as np

D_MODEL = 1024
BATCH = 1
SEQ = 256
DEPTH = 2

HEAD_DIM = 64
ROPE_THETA = 10000.0
NORM_EPS = 1e-6
Q_BLOCK = 128
D_FF = 2816
A_HEADS = 4
IDX_HEADS = 4
IDX_DIM = 64
DSA_TOPK_MAX = 256
B_HEADS = 4
MOBA_BLOCK = 256
MOBA_TOPK = 3
C_HEADS = 8
C_GROUPS = 2
C_REP = C_HEADS // C_GROUPS
CMP_BLOCK = 32
CMP_STRIDE = 16
CMP_HIDDEN = 128
SLC_BLOCK = 64
SLC_TOPN = 16
WINDOW = 512
FORCE_SCORE = 1e30
N_BRANCH = 3
A_WIDTH = A_HEADS * HEAD_DIM
B_WIDTH = B_HEADS * HEAD_DIM
C_WIDTH = C_HEADS * HEAD_DIM
IN_SIZES = (A_WIDTH, 2 * HEAD_DIM, IDX_HEADS * IDX_DIM, IDX_DIM, IDX_HEADS, 3 * B_WIDTH, C_WIDTH, 6 * C_GROUPS * HEAD_DIM, 3 * C_HEADS, N_BRANCH * D_MODEL)
IN_COLS = sum(IN_SIZES)

kernel_name = 'hybrid_dsa_moba_nsa_macaron'

def _rmsnorm(x, g):
    xf = x.astype(jnp.float32)
    y = xf * lax.rsqrt(jnp.mean(xf * xf, axis=-1, keepdims=True) + NORM_EPS)
    return (y * g.astype(jnp.float32)).astype(x.dtype)

def _swiglu(x, w_gate, w_up, w_down):
    return (jax.nn.silu(x @ w_gate) * (x @ w_up)) @ w_down

def _rope(x, pos):
    half = x.shape[-1] // 2
    inv = ROPE_THETA ** (-jnp.arange(half, dtype=jnp.float32) / half)
    ang = pos.astype(jnp.float32)[:, None] * inv[None, :]
    cos = jnp.cos(ang)[:, None, :]
    sin = jnp.sin(ang)[:, None, :]
    xf = x.astype(jnp.float32)
    x1, x2 = xf[..., :half], xf[..., half:]
    return jnp.concatenate([x1 * cos - x2 * sin, x1 * sin + x2 * cos], axis=-1).astype(x.dtype)

def _masked_softmax(s, mask):
    s = jnp.where(mask, s.astype(jnp.float32), -jnp.inf)
    m = jnp.max(s, axis=-1, keepdims=True)
    m = jnp.where(jnp.isfinite(m), m, 0.0)
    p = jnp.exp(s - m)
    den = jnp.sum(p, axis=-1, keepdims=True)
    return p / jnp.where(den > 0, den, 1.0)

def _qslice(a, q0):
    return lax.dynamic_slice_in_dim(a, q0, Q_BLOCK, axis=1)

def _sweep(fn, T):
    out = lax.map(fn, jnp.arange(T // Q_BLOCK))
    nC, B, Qb, H, dh = out.shape
    return jnp.transpose(out, (1, 0, 2, 3, 4)).reshape(B, nC * Qb, H * dh)

def _dsa_attention(q, k, v, iq, ik, iw):
    T = q.shape[1]
    topk = min(DSA_TOPK_MAX, T // 4)
    kpos = jnp.arange(T)
    idx_scale = (IDX_HEADS * IDX_DIM) ** -0.5
    scale = HEAD_DIM ** -0.5
    gather = jax.vmap(lambda a, i: a[i])

    def block(c):
        q0 = c * Q_BLOCK
        tq = q0 + jnp.arange(Q_BLOCK)
        logits = jnp.einsum('bqhe,bse->bqhs', _qslice(iq, q0), ik)
        score = jnp.einsum('bqh,bqhs->bqs', _qslice(iw, q0).astype(jnp.float32), jax.nn.relu(logits).astype(jnp.float32)) * idx_scale
        score = jnp.where(kpos[None, None, :] <= tq[None, :, None], score, -jnp.inf)
        _, sel = lax.top_k(score, topk)
        k_sel = gather(k, sel)
        v_sel = gather(v, sel)
        s = jnp.einsum('bqhd,bqkd->bqhk', _qslice(q, q0), k_sel) * scale
        p = _masked_softmax(s, (sel <= tq[None, :, None])[:, :, None, :])
        return jnp.einsum('bqhk,bqkd->bqhd', p.astype(v.dtype), v_sel)

    return _sweep(block, T)

def _moba_attention(q, k, v):
    B, T, H, dh = q.shape
    scale = dh ** -0.5
    nb = max(-(-T // MOBA_BLOCK), MOBA_TOPK + 1)
    pad = ((0, 0), (0, nb * MOBA_BLOCK - T), (0, 0), (0, 0))
    kp = jnp.pad(k, pad)
    vp = jnp.pad(v, pad)
    kb = kp.reshape(B, nb, MOBA_BLOCK, H, dh)
    kmean = jnp.mean(kb.astype(jnp.float32), axis=2)
    kbh = jnp.transpose(kb, (0, 3, 1, 2, 4))
    vbh = jnp.transpose(vp.reshape(B, nb, MOBA_BLOCK, H, dh), (0, 3, 1, 2, 4))
    bi = jnp.arange(B)[:, None, None, None]
    hi = jnp.arange(H)[None, None, :, None]
    blk = jnp.arange(nb)

    def block(c):
        q0 = c * Q_BLOCK
        tq = q0 + jnp.arange(Q_BLOCK)
        own = q0 // MOBA_BLOCK
        qc = _qslice(q, q0)
        gate = jnp.einsum('bqhd,bnhd->bqhn', qc.astype(jnp.float32), kmean)
        gate = jnp.where(blk < own, gate, -jnp.inf)
        _, sel = lax.top_k(gate, MOBA_TOPK)
        k_sel = kbh[bi, hi, sel]
        v_sel = vbh[bi, hi, sel].reshape(B, Q_BLOCK, H, MOBA_TOPK * MOBA_BLOCK, dh)
        s_sel = jnp.einsum('bqhd,bqhjsd->bqhjs', qc, k_sel).reshape(B, Q_BLOCK, H, MOBA_TOPK * MOBA_BLOCK)
        m_sel = jnp.repeat(sel < own, MOBA_BLOCK, axis=-1)
        k_own = lax.dynamic_slice_in_dim(kp, own * MOBA_BLOCK, MOBA_BLOCK, axis=1)
        v_own = lax.dynamic_slice_in_dim(vp, own * MOBA_BLOCK, MOBA_BLOCK, axis=1)
        s_own = jnp.einsum('bqhd,bshd->bqhs', qc, k_own)
        m_own = (own * MOBA_BLOCK + jnp.arange(MOBA_BLOCK))[None, :] <= tq[:, None]
        s = jnp.concatenate([s_sel, s_own], axis=-1) * scale
        mask = jnp.concatenate([m_sel, jnp.broadcast_to(m_own[None, :, None, :], (B, Q_BLOCK, H, MOBA_BLOCK))], axis=-1)
        p = _masked_softmax(s, mask).astype(v.dtype)
        n_sel_keys = MOBA_TOPK * MOBA_BLOCK
        return (jnp.einsum('bqhm,bqhmd->bqhd', p[..., :n_sel_keys], v_sel)
                + jnp.einsum('bqhs,bshd->bqhd', p[..., n_sel_keys:], v_own))

    return _sweep(block, T)

def _compress(kv, pos_emb, w1, w2):
    B, T, G, dh = kv.shape
    nc = (T - CMP_BLOCK) // CMP_STRIDE + 1
    idx = jnp.arange(nc)[:, None] * CMP_STRIDE + jnp.arange(CMP_BLOCK)[None, :]
    blk = kv[:, idx] + pos_emb[:, None, :]
    flat = jnp.transpose(blk, (0, 1, 3, 2, 4)).reshape(B, nc, G, CMP_BLOCK * dh)
    return jax.nn.gelu(flat @ w1) @ w2

def _nsa_attention(q_raw, q_rot, k_cmp, v_cmp, k_slc, v_slc, k_win, v_win, gates):
    B, T = q_raw.shape[0], q_raw.shape[1]
    G, R, dh = C_GROUPS, C_REP, HEAD_DIM
    scale = dh ** -0.5
    nc = k_cmp.shape[1]
    ns = T // SLC_BLOCK
    n_sel = min(SLC_TOPN, ns)
    cmp_start = jnp.arange(nc) * CMP_STRIDE
    cmp_last = cmp_start + CMP_BLOCK - 1
    slc_start = jnp.arange(ns) * SLC_BLOCK
    overlap = ((cmp_start[:, None] < slc_start[None, :] + SLC_BLOCK) & (slc_start[None, :] <= cmp_last[:, None])).astype(jnp.float32)
    blk = jnp.arange(ns)
    k_sb = jnp.transpose(k_slc.reshape(B, ns, SLC_BLOCK, G, dh), (0, 3, 1, 2, 4))
    v_sb = jnp.transpose(v_slc.reshape(B, ns, SLC_BLOCK, G, dh), (0, 3, 1, 2, 4))
    wpad = ((0, 0), (WINDOW, 0), (0, 0), (0, 0))
    k_wp = jnp.pad(k_win, wpad)
    v_wp = jnp.pad(v_win, wpad)
    win_off = jnp.arange(WINDOW + Q_BLOCK) - WINDOW
    bi = jnp.arange(B)[:, None, None, None]
    gi = jnp.arange(G)[None, None, :, None]

    def block(c):
        q0 = c * Q_BLOCK
        tq = q0 + jnp.arange(Q_BLOCK)
        qn = _qslice(q_raw, q0).reshape(B, Q_BLOCK, G, R, dh)
        qr = _qslice(q_rot, q0).reshape(B, Q_BLOCK, G, R, dh)
        s_c = jnp.einsum('bqgrd,bngd->bqgrn', qn, k_cmp) * scale
        p_c = _masked_softmax(s_c, (cmp_last[None, :] <= tq[:, None])[None, :, None, None, :])
        o_c = jnp.einsum('bqgrn,bngd->bqgrd', p_c.astype(v_cmp.dtype), v_cmp)
        imp = jnp.einsum('bqgrn,nj->bqgj', p_c, overlap)
        jq = tq // SLC_BLOCK
        adm = blk[None, :] <= jq[:, None]
        forced = (blk[None, :] == 0) | (blk[None, :] == jq[:, None]) | (blk[None, :] == jq[:, None] - 1)
        score = jnp.where(adm[None, :, None, :], imp, -jnp.inf)
        score = jnp.where((adm & forced)[None, :, None, :], FORCE_SCORE, score)
        _, sel = lax.top_k(score, n_sel)
        k_sel = k_sb[bi, gi, sel]
        v_sel = v_sb[bi, gi, sel].reshape(B, Q_BLOCK, G, n_sel * SLC_BLOCK, dh)
        s_s = jnp.einsum('bqgrd,bqgjsd->bqgrjs', qr, k_sel).reshape(B, Q_BLOCK, G, R, n_sel * SLC_BLOCK) * scale
        kpos = (sel[..., None] * SLC_BLOCK + jnp.arange(SLC_BLOCK)).reshape(B, Q_BLOCK, G, n_sel * SLC_BLOCK)
        p_s = _masked_softmax(s_s, (kpos <= tq[None, :, None, None])[:, :, :, None, :])
        o_s = jnp.einsum('bqgrm,bqgmd->bqgrd', p_s.astype(v_slc.dtype), v_sel)
        k_wc = lax.dynamic_slice_in_dim(k_wp, q0, WINDOW + Q_BLOCK, axis=1)
        v_wc = lax.dynamic_slice_in_dim(v_wp, q0, WINDOW + Q_BLOCK, axis=1)
        kpos_w = q0 + win_off
        diff = tq[:, None] - kpos_w[None, :]
        mask_w = (diff >= 0) & (diff < WINDOW) & (kpos_w[None, :] >= 0)
        s_w = jnp.einsum('bqgrd,bkgd->bqgrk', qr, k_wc) * scale
        p_w = _masked_softmax(s_w, mask_w[None, :, None, None, :])
        o_w = jnp.einsum('bqgrk,bkgd->bqgrd', p_w.astype(v_win.dtype), v_wc)
        g = _qslice(gates, q0).reshape(B, Q_BLOCK, G, R, 3)
        o = g[..., 0:1] * o_c + g[..., 1:2] * o_s + g[..., 2:3] * o_w
        return o.reshape(B, Q_BLOCK, C_HEADS, dh)

    return _sweep(block, T)

def setup_inputs(seed: int = 0) -> dict:
    key = jax.random.key(seed)
    k = jax.random.split(key, 22)
    L, D = DEPTH, D_MODEL

    def nrm(kk, shape, fan_in):
        return jax.random.normal(kk, shape, jnp.float32) * (fan_in ** -0.5)

    def gain(kk, shape):
        return 1.0 + 0.05 * jax.random.normal(kk, shape, jnp.float32)

    cmp_in = CMP_BLOCK * HEAD_DIM
    return {
        'x': jax.random.normal(k[0], (BATCH, SEQ, D), jnp.float32),
        'ffn1_norm': gain(k[1], (L, D)),
        'ffn1_w_gate': nrm(k[2], (L, D, D_FF), D),
        'ffn1_w_up': nrm(k[3], (L, D, D_FF), D),
        'ffn1_w_down': nrm(k[4], (L, D_FF, D), D_FF),
        'mix_norm': gain(k[5], (L, D)),
        'w_in': nrm(k[6], (L, D, IN_COLS), D),
        'cmp_pos_k': 0.1 * jax.random.normal(k[7], (L, CMP_BLOCK, HEAD_DIM), jnp.float32),
        'cmp_w1_k': nrm(k[8], (L, cmp_in, CMP_HIDDEN), cmp_in),
        'cmp_w2_k': nrm(k[9], (L, CMP_HIDDEN, HEAD_DIM), CMP_HIDDEN),
        'cmp_pos_v': 0.1 * jax.random.normal(k[10], (L, CMP_BLOCK, HEAD_DIM), jnp.float32),
        'cmp_w1_v': nrm(k[11], (L, cmp_in, CMP_HIDDEN), cmp_in),
        'cmp_w2_v': nrm(k[12], (L, CMP_HIDDEN, HEAD_DIM), CMP_HIDDEN),
        'w_branch_a': nrm(k[13], (L, A_WIDTH, D), A_WIDTH),
        'w_branch_b': nrm(k[14], (L, B_WIDTH, D), B_WIDTH),
        'w_branch_c': nrm(k[15], (L, C_WIDTH, D), C_WIDTH),
        'w_out': nrm(k[16], (L, D, D), D),
        'ffn2_norm': gain(k[17], (L, D)),
        'ffn2_w_gate': nrm(k[18], (L, D, D_FF), D),
        'ffn2_w_up': nrm(k[19], (L, D, D_FF), D),
        'ffn2_w_down': nrm(k[20], (L, D_FF, D), D_FF),
        'final_norm': gain(k[21], (D,)),
    }

def reference(x, ffn1_norm, ffn1_w_gate, ffn1_w_up, ffn1_w_down, mix_norm, w_in,
              cmp_pos_k, cmp_w1_k, cmp_w2_k, cmp_pos_v, cmp_w1_v, cmp_w2_v,
              w_branch_a, w_branch_b, w_branch_c, w_out,
              ffn2_norm, ffn2_w_gate, ffn2_w_up, ffn2_w_down, final_norm):
    B, T, D = x.shape
    pos = jnp.arange(T)
    cuts = np.cumsum(IN_SIZES)[:-1].tolist()
    for l in range(DEPTH):
        x = x + 0.5 * _swiglu(_rmsnorm(x, ffn1_norm[l]), ffn1_w_gate[l], ffn1_w_up[l], ffn1_w_down[l])
        h = _rmsnorm(x, mix_norm[l])
        a_q, a_kv, i_q, i_k, i_w, b_qkv, c_q, c_kv, c_g, m_g = jnp.split(h @ w_in[l], cuts, axis=-1)
        a_q = _rope(a_q.reshape(B, T, A_HEADS, HEAD_DIM), pos)
        a_k = _rope(a_kv[..., None, :HEAD_DIM], pos)[:, :, 0]
        a_v = a_kv[..., HEAD_DIM:]
        i_q = _rope(i_q.reshape(B, T, IDX_HEADS, IDX_DIM), pos)
        i_k = _rope(i_k[:, :, None, :], pos)[:, :, 0]
        y_a = _dsa_attention(a_q, a_k, a_v, i_q, i_k, i_w) @ w_branch_a[l]
        b_qkv = b_qkv.reshape(B, T, 3, B_HEADS, HEAD_DIM)
        y_b = _moba_attention(_rope(b_qkv[:, :, 0], pos), _rope(b_qkv[:, :, 1], pos), b_qkv[:, :, 2]) @ w_branch_b[l]
        c_q = c_q.reshape(B, T, C_HEADS, HEAD_DIM)
        c_kv = c_kv.reshape(B, T, 6, C_GROUPS, HEAD_DIM)
        k_cmp = _compress(c_kv[:, :, 0], cmp_pos_k[l], cmp_w1_k[l], cmp_w2_k[l])
        v_cmp = _compress(c_kv[:, :, 1], cmp_pos_v[l], cmp_w1_v[l], cmp_w2_v[l])
        c_gates = jax.nn.sigmoid(c_g.reshape(B, T, C_HEADS, 3))
        y_c = _nsa_attention(c_q, _rope(c_q, pos), k_cmp, v_cmp,
                             _rope(c_kv[:, :, 2], pos), c_kv[:, :, 3],
                             _rope(c_kv[:, :, 4], pos), c_kv[:, :, 5], c_gates) @ w_branch_c[l]
        g = jax.nn.sigmoid(m_g.reshape(B, T, N_BRANCH, D))
        x = x + (g[:, :, 0] * y_a + g[:, :, 1] * y_b + g[:, :, 2] * y_c) @ w_out[l]
        x = x + 0.5 * _swiglu(_rmsnorm(x, ffn2_norm[l]), ffn2_w_gate[l], ffn2_w_up[l], ffn2_w_down[l])
    return _rmsnorm(x, final_norm)


_drawn_inputs = setup_inputs


def setup_inputs(seed=0):
    import zlib

    import numpy as np

    out = dict(_drawn_inputs(seed))
    spreads = {}
    factors = {'cmp_pos_k': 8.0}
    for name, (base, spread) in spreads.items():
        noise = np.random.default_rng([zlib.crc32(name.encode()), seed]).standard_normal(out[name].shape)
        drawn = base * np.exp(spread * noise) if base else spread * noise
        out[name] = jnp.asarray(drawn.astype(out[name].dtype))
    for name, factor in factors.items():
        out[name] = (out[name] * factor).astype(out[name].dtype)
    return out
```

```python
from contextlib import ExitStack

import numpy as np

import concourse.bass as bass
from concourse import mybir

F32 = mybir.dt.float32
F32R = mybir.dt.float32r
BF16 = mybir.dt.bfloat16
ALU = mybir.AluOpType
ACT = mybir.ActivationFunctionType
AX_X = mybir.AxisListType.X
ds = bass.ds

P = 128
SEQ, D, DFF, DEPTH = 256, 1024, 2816, 2
NT = SEQ // P
KD = D // P
HD = 64
EPS = 1e-6
ATT_SCALE = HD ** -0.5
IDX_SCALE = (4 * HD) ** -0.5
TOPK = SEQ // 4
NCMP, CMP_STRIDE, CMP_BLOCK = 15, 16, 32
CPAD = 16
BIG = 1e30
FILL = -3.0e38
TAKEN = -3.4e38

A_Q, A_K, A_V, I_Q, I_K, I_W = 0, 256, 320, 384, 640, 704
B_Q, B_K, B_V, C_Q = 708, 964, 1220, 1476
C_KC, C_VC, C_KS, C_VS, C_KW, C_VW, C_G, M_G = 1988, 2116, 2244, 2372, 2500, 2628, 2756, 2780
NPROJ = M_G
LASTU = NPROJ - 5 * 512

SLAB = 2048
FSTEP = 256
NSTEP = DFF // FSTEP
FFN_SLABS = 3 * NSTEP
MIX_SLABS = 33
LAYER_SLABS = 2 * FFN_SLABS + MIX_SLABS
M_CK, M_CV = 13, 14
S_CK, S_CV = FFN_SLABS + M_CK, FFN_SLABS + M_CV
LAYER_SPLITS = LAYER_SLABS - 2
M_BR, M_WO = 25, 29

QBLK = {"A": 0, "I": 2, "B": 4, "R": 6}
KBLK = {"A": 0, "I": 1, "B": 2, "S": 4, "W": 6}
NQB, NKB, NRB = 10, 8, 18
ROPE = {
    0: [(A_Q, 4, 0, False), (A_K, 1, 2, True)],
    1: [(I_Q, 4, 3, False), (I_K, 1, 5, True), (B_Q, 4, 6, False)],
    2: [(B_K, 4, 8, False)],
    3: [(C_Q, 8, 10, False)],
    4: [(C_KS, 2, 14, True)],
    5: [(C_KW, 2, 16, True)],
}
FILLS = [((0, 1), ("qs", 0), ("qs", 1)), ((2, 3), ("k", 0), ("q", 2)), ((4, 5), ("q", 3), ("k", 1)),
         ((6, 7), ("qs", 4), ("qs", 5)), ((8, 9), ("k", 2), ("k", 3)), ((10, 11), ("qs", 6), ("qs", 7)),
         ((12, 13), ("qs", 8), ("qs", 9)), ((14, 15), ("k", 4), ("k", 5)), ((16, 17), ("k", 6), ("k", 7)),
         ((18, 19), ("n", 0), ("n", 1)), ((20, 21), ("n", 2), ("n", 3))]
NFILL = len(FILLS) + 2
T1 = 5

PAIRS = ["I", "C", "B", "S0", "S1", "W0", "W1", "A"]
NPOS = len(PAIRS) + 2
V_STEPS = 184
SETUP_G = 18


def build(nc, x_in, ffn1_norm, ffn1_w_gate, ffn1_w_up, ffn1_w_down, mix_norm, w_in, cmp_pos_k, cmp_w1_k,
          cmp_w2_k, cmp_pos_v, cmp_w1_v, cmp_w2_v, w_branch_a, w_branch_b, w_branch_c, w_out, ffn2_norm,
          ffn2_w_gate, ffn2_w_up, ffn2_w_down, final_norm, cos_t, sin_t, out):
    ctx = ExitStack()
    with ctx:
        def sb(name, shape, dt=F32):
            return ctx.enter_context(nc.sbuf_tensor(name, shape, dt))

        def sem(name):
            return ctx.enter_context(nc.semaphore(name))

        raw = sb("raw", [P, 3, SLAB])
        whi = sb("whi", [P, 3, SLAB], F32R)
        wlo = sb("wlo", [P, 3, SLAB], F32R)
        x = sb("x", [P, NT, D])
        ht_hi = sb("ht_hi", [P, KD, SEQ], F32R)
        ht_lo = sb("ht_lo", [P, KD, SEQ], F32R)
        at_hi = sb("at_hi", [P, 2, SEQ], F32R)
        at_lo = sb("at_lo", [P, 2, SEQ], F32R)
        scr = sb("scr", [P, 4 * SEQ])
        sg = scr[:, 0:512].rearrange("p (t c) -> p t c", t=NT)
        act = scr[:, 512:1024].rearrange("p (t c) -> p t c", t=NT)
        kvs = scr[:, :].rearrange("p (v g c) -> p v g c", v=2, g=2)
        pr = sb("proj", [P, NT, NPROJ])
        gr = sb("gates", [P, NT * 3 * D])
        gate = gr[:, :].rearrange("p (t b c) -> p t b c", t=NT, b=3)
        rs = gr[:, 0:NT * NRB * P].rearrange("p (t b c) -> p t b c", t=NT, b=NRB)
        cmpm = gr[:, NT * NRB * P:NT * NRB * P + 1024].rearrange("p (v j c) -> p v j c", v=2, j=16)
        q_t = sb("q_t", [P, NQB, SEQ])
        k_t = sb("k_t", [P, NKB, 2, SEQ])
        prob = sb("prob", [P, 2, 1536])
        qn_t = prob[:, 1, 512:1536].rearrange("p (b c) -> p b c", b=4)
        p_t = sb("p_t", [P, 3, 512])
        cos_s = sb("cos_s", [P, NT, HD])
        sin_s = sb("sin_s", [P, NT, HD])
        rtmp = prob[:, 0, 0:NT * 8 * HD].rearrange("p (t h c) -> p t h c", t=NT, h=8)
        ident = sb("ident", [P, P])
        ident_b = sb("ident_b", [P, P], BF16)
        cmask = sb("cmask", [P, NT, SEQ])
        cmask_b = sb("cmask_b", [P, NT, SEQ], BF16)
        kmask_b = sb("kmask_b", [P, NT, CPAD], BF16)
        valid = sb("valid", [P, NT])
        hsel = sb("hsel", [P, 8])
        rows = sb("rows", [112, P])
        cols = sb("cols", [P, 112])
        w2_all = sb("w2_all", [P, DEPTH, 3, HD])
        cur = sb("cur", [P, 3 * KD + 32 + 3 * HD])
        ssq = sb("ssq", [P, NT])
        msq = sb("msq", [P, NT])
        mhalf = sb("mhalf", [P, NT])
        rstd = sb("rstd", [P, NT])
        hrstd = sb("hrstd", [P, NT])
        work = sb("work", [P, 384])
        top8 = sb("top8", [P, 8])
        sel_b = sb("sel_b", [P, 384], BF16)
        nmax = sb("nmax", [P, 2, 16])
        den = sb("den", [P, 2, 16])
        rden = sb("rden", [P, 2, 16])
        cgt = sb("cgt", [P, NT, 24])
        cgt3 = cgt[:, :, :].rearrange("p t (h b) -> p t h b", b=3)
        hid = sb("hid", [P, 64])
        hid2 = sb("hid2", [P, 64])
        hid3 = sb("hid3", [P, 64])
        hid_v = sb("hid_v", [P, 8, CPAD])
        kc_t = sb("kc_t", [P, 2, 2, CPAD])
        comb = scr[:, 0:512].rearrange("p (h c) -> p h c", h=8)
        v_blk = scr[:, 512:1024].rearrange("p (h c) -> p h c", h=8)
        ps = ctx.enter_context(nc.psum_tensor("ps", [P, 8, 512], F32))

        gains = cur[:, 0:3 * KD]
        pos_c = cur[:, 3 * KD:3 * KD + 32].rearrange("p (v j) -> p v j", v=2)
        w2k = cur[:, 3 * KD + 32:3 * KD + 32 + 2 * HD]
        w2v = cur[:, 3 * KD + 32 + 2 * HD:]

        raw_in = [sem(f"raw_in{n}") for n in range(3)]
        hi_done = sem("hi_done")
        lo_done = sem("lo_done")
        slab_used = sem("slab_used")
        waited = sem("waited")
        x_loaded = sem("x_loaded")
        small_in = sem("small_in")
        setup_pe = sem("setup_pe")
        setup_v = sem("setup_v")
        setup_g = sem("setup_g")
        setup_w = sem("setup_w")
        cur_ready = sem("cur_ready")
        x_new = sem("x_new")
        xt_ps = sem("xt_ps")
        hth = sem("hth")
        htl = sem("htl")
        ssq_done = sem("ssq_done")
        rstd_ready = sem("rstd_ready")
        sub_out = sem("sub_out")
        silu_done = sem("silu_done")
        act_done = sem("act_done")
        at_ps = sem("at_ps")
        ath = sem("ath")
        atl = sem("atl")
        proj_done = sem("proj_done")
        fill_ps = sem("fill_ps")
        fill_a = sem("fill_a")
        v_step = sem("v_step")
        cg_done = sem("cg_done")
        cmp_ps = sem("cmp_ps")
        gelu_t = sem("gelu_t")
        gate_t = sem("gate_t")
        gate_ready = sem("gate_ready")
        sc_ps = sem("sc_ps")
        exp_done = sem("exp_done")
        pt_ps = sem("pt_ps")
        pt_a = sem("pt_a")
        o_ps = sem("o_ps")
        ot_ps = sem("ot_ps")
        ot_h = sem("ot_h")
        y_ps = sem("y_ps")
        zsum = sem("zsum")
        out_done = sem("out_done")

        at_step = {}
        
        def of(s):
            return s if isinstance(s, tuple) else (0, s)

        def slot(s):
            return of(s)[1] % 3

        def wait_raw(eng, l, s):
            i, c = of(s)
            eng.wait_ge(raw_in[c % 3], l * (32 * LAYER_SLABS // 3) + i * 32 + 32 * (c // 3 + 1))

        def wait_used(eng, l, s):
            i, c = of(s)
            eng.wait_ge(slab_used, l * LAYER_SLABS + i * 3 + (c + 1 + 3))

        def splits(c):
            return c - (c > S_CK) - (c > S_CV)

        def wait_hi(eng, l, s):
            i, c = of(s)
            eng.wait_ge(hi_done, l * LAYER_SPLITS + i * 3 + splits(c) + 1)

        def wait_lo(eng, l, s):
            i, c = of(s)
            eng.wait_ge(lo_done, l * LAYER_SPLITS + i * 3 + splits(c) + 1 + 3)

        def apart(eng):
            eng.sem_inc(waited, 1)

        def wait_step(eng, l, name):
            eng.wait_ge(v_step, l * V_STEPS + at_step[name])

        def score_views(t):
            if t == 0:
                return ps[:, 4, :].rearrange("p (h c) -> p h c", h=4)
            return ps[:, 2:4, :].rearrange("p b (h c) -> p (b h) c", h=2)

        def prob_view(b, t):
            a, w = (0, P) if t == 0 else (512, SEQ)
            return prob[:, b, a:a + 4 * w].rearrange("p (h c) -> p h c", h=4)

        def heads_of(pair):
            if pair == "A":
                return QBLK["A"], KBLK["A"], 0, lambda h: A_V, A_Q
            if pair == "I":
                return QBLK["I"], KBLK["I"], 0, None, None
            if pair == "B":
                return QBLK["B"], KBLK["B"], 1, lambda h: B_V + h * HD, B_Q
            g = int(pair[1])
            v = C_VS if pair[0] == "S" else C_VW
            return QBLK["R"] + 2 * g, KBLK[pair[0]] + g, 0, lambda h: v + g * HD, C_Q + g * 4 * HD

        PT_FILLS = [(0, 0), (1, 0), (1, 1)]

        def fills_before(e):
            return 0 if e <= 1 else 1 + 3 * (e - 2)

        PT_LAYER = fills_before(len(PAIRS))

        PT_ACT = 1 + 2 * (len(PAIRS) - 2)

        def acts_before(e):
            return 0 if e <= 1 else 1 + 2 * (e - 2)

        def copy_fill(copy, f):
            bank = 4 + f % 4
            if f >= len(FILLS):
                v = f - len(FILLS)
                src = ps[:, bank, :].rearrange("p (g c) -> p g c", g=2)
                copy(kvs[0:64, v, :, :], src[0:64], 1.0)
                copy(kvs[64:P, v, :, 0:SEQ - 1], src[64:P, :, 1:SEQ], 1.0)
                return
            (k0, b0), (k1, b1) = FILLS[f][1:]
            if k0 == "n":
                copy(qn_t[:, b0:b0 + 2, :].rearrange("p b c -> p (b c)"), ps[:, bank, :], ATT_SCALE)
                return
            if k0 == k1 != "k":
                copy(q_t[:, b0:b0 + 2, :].rearrange("p b c -> p (b c)"), ps[:, bank, :], ATT_SCALE if k0 == "qs" else 1.0)
                return
            for j, (kind, b) in enumerate(FILLS[f][1:]):
                src = ps[:, bank, j * SEQ:(j + 1) * SEQ]
                if kind == "k":
                    copy(k_t[0:64, b, 0, :], src[0:64], 1.0)
                    copy(k_t[64:P, b, 1, :], src[64:P], 1.0)
                else:
                    copy(q_t[:, b, :], src, ATT_SCALE if kind == "qs" else 1.0)

        def small_loads():
            for n, w in enumerate((ffn1_norm, mix_norm, ffn2_norm)):
                yield rows[16 * n:16 * n + 16, :], w.rearrange("l (k p) -> (l k) p", p=P)
            for v, w in enumerate((cmp_pos_k, cmp_pos_v)):
                yield rows[48 + 32 * v:80 + 32 * v, :], w.rearrange("l (j h) d -> (l j) (h d)", h=2)
            for n, w in enumerate((cmp_w2_k, cmp_w2_k, cmp_w2_v)):
                yield w2_all[:, :, n, :], w.rearrange("l p d -> p l d")
            yield cos_s[:, :, :], cos_t.rearrange("(t p) c -> p t c", p=P)
            yield sin_s[:, :, :], sin_t.rearrange("(t p) c -> p t c", p=P)

        SMALL_DMAS = 10

        block = ctx.enter_context(nc.Block())

        @block.vector
        def _(dve):
            count = [0]

            def step(ins, name=None):
                count[0] += 1
                ins.then_inc(v_step, 1)
                if name is not None:
                    at_step[name] = count[0]

            def own(l):
                dve.wait_ge(v_step, l * V_STEPS + count[0])

            def convert(l, s, w=SLAB):
                wait_raw(dve, l, s)
                wait_hi(dve, l, s)
                i, c = of(s)
                wait_used(dve, l, (i, c - 3))
                n = slot(s)
                nc.vector.tensor_tensor(wlo[:, n, 0:w], raw[:, n, 0:w], whi[:, n, 0:w].bitcast(F32),
                                        ALU.subtract).then_inc(lo_done, 1)

            def prep(l, n, banks):
                for k in range(KD):
                    if k % 2 == 0:
                        dve.wait_ge(hth, (l * 3 + n) * KD + k + 2)
                    src = ps[:, banks[(k // 2) % 2], (k % 2) * SEQ:(k % 2 + 1) * SEQ]
                    nc.vector.scalar_tensor_tensor(ht_lo[:, k, :], src, gains[:, n * KD + k:n * KD + k + 1],
                                                   ht_hi[:, k, :].bitcast(F32), ALU.mult,
                                                   ALU.subtract).then_inc(htl, 1)

            def residual(l, n, bank0, factor, last_slab):
                for g in range(4):
                    half, t = g // 2, g % 2
                    if g < 3:
                        dve.wait_ge(sub_out, (l * 3 + n) * 3 + g + 1)
                    else:
                        wait_used(dve, l, last_slab)
                    xv = x[:, t, half * 512:(half + 1) * 512]
                    nc.vector.scalar_tensor_tensor(xv, ps[:, bank0 + g, :], factor, xv, ALU.mult,
                                                   ALU.add).then_inc(x_new, 1)

            def products(l, f, i):
                r = l * 2 + f
                for t in range(NT):
                    dve.wait_ge(silu_done, r * (2 * NSTEP) + i * 2 + t + 1)
                    if not (isinstance(i, int) and i == 0):
                        dve.wait_ge(at_ps, r * NSTEP + i)
                    nc.vector.scalar_tensor_tensor(act[:, t, :], ps[:, t, FSTEP:2 * FSTEP], rstd[:, t:t + 1],
                                                   sg[:, t, :], ALU.mult, ALU.mult).then_inc(act_done, 1)

            def act_rest(l, f, i):
                dve.wait_ge(ath, (l * 2 + f) * NSTEP + i + 1)
                nc.vector.tensor_tensor(at_lo[:, :, :].rearrange("p j c -> p (j c)"), ps[:, 2, :],
                                        at_hi[:, :, :].rearrange("p j c -> p (j c)").bitcast(F32),
                                        ALU.subtract).then_inc(atl, 1)

            def ffn(l, f):
                n, s0 = 2 * f, f * (FFN_SLABS + MIX_SLABS)
                if f == 0:
                    dve.wait_ge(cur_ready, l * 3 + 3)
                prep(l, n, (2, 3) if f == 0 else (4, 5))
                convert(l, s0 + 2)
                dve.wait_ge(rstd_ready, (l * 3 + n) * 3 + 3)
                products(l, f, 0)
                convert(l, s0 + 3)
                act_rest(l, f, 0)
                with dve.Fori(1, NSTEP) as i:
                    convert(l, (i, s0 + 1))
                    convert(l, (i, s0 + 2))
                    products(l, f, i)
                    convert(l, (i, s0 + 3))
                    act_rest(l, f, i)
                convert(l, s0 + FFN_SLABS + 1)
                residual(l, n, 4, 0.5, s0 + FFN_SLABS - 1)

            def rope(l, u):
                dve.wait_ge(proj_done, l * 12 + 2 * u + 2)
                for c0, nh, b0, dup in ROPE[u]:
                    src = pr[:, :, c0:c0 + nh * HD].rearrange("p t (h c) -> p t h c", h=nh)
                    if dup:
                        dst = rs[:, :, b0:b0 + nh, 0:HD]
                    else:
                        dst = rs[:, :, b0:b0 + nh // 2, :].rearrange("p t b (e c) -> p t (b e) c", e=2)
                    tmp = rtmp[:, :, 0:nh, :]
                    cb = cos_s[:, :, :].unsqueeze(2).broadcast_to([P, NT, nh, HD])
                    sb_ = sin_s[:, :, :].unsqueeze(2).broadcast_to([P, NT, nh, HD])
                    own(l)
                    step(nc.vector.tensor_tensor(dst, src, cb, ALU.mult))
                    step(nc.vector.tensor_tensor(tmp[:, :, :, 0:32], src[:, :, :, 32:64], sb_[:, :, :, 0:32],
                                                 ALU.mult))
                    step(nc.vector.tensor_tensor(tmp[:, :, :, 32:64], src[:, :, :, 0:32], sb_[:, :, :, 32:64],
                                                 ALU.mult))
                    own(l)
                    step(nc.vector.tensor_tensor(dst, dst, tmp, ALU.add))
                    if dup:
                        own(l)
                        step(nc.vector.tensor_copy(rs[:, :, b0:b0 + nh, HD:2 * HD], dst))
                at_step["rope", u] = count[0]

            def fill_out(l, f):
                dve.wait_ge(fill_ps, l * NFILL + f + 1)
                copy_fill(lambda o, i, k: step(nc.vector.tensor_scalar(o, i, k, None, ALU.mult)), f)
                at_step["fill", f] = count[0]

            def cmp_windows(l):
                dve.wait_ge(fill_a, l * 7 + 7)
                own(l)
                for v in range(2):
                    for g in range(2):
                        for a in range(2):
                            win = kvs[:, v, g, 16 * a:16 * a + CMP_STRIDE * NCMP]\
                                .rearrange("p (n j r) -> p j n r", j=8, r=2)[:, :, :, 0]
                            o = cmpm[:, v, 8 * a:8 * a + 8, g * CPAD:g * CPAD + NCMP]
                            pb = pos_c[:, v, 8 * a:8 * a + 8].unsqueeze(2).broadcast_to([P, 8, NCMP])
                            step(nc.vector.tensor_tensor(o, win, pb, ALU.add), ("windows",))

            def compress(l):
                wait_used(dve, l, S_CV)
                own(l)
                step(nc.vector.tensor_copy(hid[:, :], ps[:, 7, 0:64]))
                own(l)
                step(nc.vector.tensor_tensor(hid2[:, :], hid[:, :], hid[:, :], ALU.mult))
                own(l)
                step(nc.vector.tensor_scalar(hid2[:, :], hid2[:, :], 0.044715, 1.0, ALU.mult, ALU.add))
                own(l)
                step(nc.vector.tensor_tensor(hid2[:, :], hid2[:, :], hid[:, :], ALU.mult), ("gelu arg",))
                dve.wait_ge(gelu_t, l + 1)
                step(nc.vector.scalar_tensor_tensor(hid2[:, :], hid3[:, :], 1.0, hid[:, :], ALU.add, ALU.mult))
                own(l)
                step(nc.vector.tensor_scalar(hid[:, 0:32], hid2[:, 0:32], 0.5, None, ALU.mult))
                for g in range(2):
                    hv = hid2[:, 32 + g * CPAD:32 + (g + 1) * CPAD].unsqueeze(1).broadcast_to([P, 4, CPAD])
                    step(nc.vector.tensor_scalar(hid_v[:, 4 * g:4 * g + 4, :], hv, 0.5, None, ALU.mult),
                         ("hidden",))

            def compressed_out(l):
                dve.wait_ge(cmp_ps, l * 2 + 2)
                src = ps[:, 7, 64:96].rearrange("p (g c) -> p g c", g=2)
                step(nc.vector.tensor_copy(kc_t[0:64, :, 0, :], src[0:64]))
                step(nc.vector.tensor_copy(kc_t[64:P, :, 1, :], src[64:P]), ("kc",))
                vb = ps[:, 7, 96:160].unsqueeze(1).broadcast_to([P, 8, HD])
                step(nc.vector.tensor_tensor(v_blk[:, :, :], vb, hsel[:, :].unsqueeze(2).broadcast_to([P, 8, HD]),
                                             ALU.mult), ("v_blk",))

            def maxima(l, e):
                pair, b = PAIRS[e], e % 2
                own(l)
                for t in range(NT):
                    dve.wait_ge(sc_ps, l * 16 + 2 * e + t + 1)
                    if pair == "C":
                        continue
                    step(nc.vector.tensor_reduce(nmax[:, b, 4 * t:4 * t + 4], score_views(t), AX_X, ALU.max,
                                                 negate=True), ("max", e))
                if pair == "C":
                    sc = ps[:, 4, 0:256].rearrange("p (h c) -> p h c", h=16)
                    step(nc.vector.tensor_reduce(nmax[:, b, :], sc, AX_X, ALU.max, negate=True))
                    own(l)
                    o = prob[:, b, 0:256].rearrange("p (h c) -> p h c", h=16)
                    step(nc.vector.tensor_tensor(o, sc, nmax[:, b, :].unsqueeze(2).broadcast_to([P, 16, CPAD]),
                                                 ALU.add), ("max", e))

            def normed(l, e):
                pair, b = PAIRS[e], e % 2
                dve.wait_ge(o_ps, l * 7 + e)
                own(l)
                if pair == "C":
                    src = prob[:, b, 0:256].rearrange("p (h c) -> p h c", h=16)
                    step(nc.vector.tensor_reduce(den[:, b, :], src, AX_X, ALU.add))
                    own(l)
                    step(nc.vector.reciprocal(rden[:, b, :], den[:, b, :]))
                    own(l)
                    rt = rden[:, b, :].rearrange("p (t h) -> p t h", t=NT)
                    step(nc.vector.tensor_tensor(rt, rt, cgt3[:, :, :, 0], ALU.mult))
                    own(l)
                    for t in range(NT):
                        o = pr[:, t, C_Q:C_Q + 512].rearrange("p (h c) -> p h c", h=8)
                        i = ps[:, 7 - t, :].rearrange("p (h c) -> p h c", h=8)
                        step(nc.vector.tensor_tensor(o, i, rt[:, t, :].unsqueeze(2).broadcast_to([P, 8, HD]),
                                                     ALU.mult), ("norm", e))
                    return
                _, _, _, _, oc = heads_of(pair)
                rd = rden[:, b, 0:8]
                step(nc.vector.reciprocal(rd, den[:, b, 0:8]))
                own(l)
                o_in = ps[:, 7, :].rearrange("p (x c) -> p x c", c=HD)
                if pair in "AB":
                    o = pr[:, :, oc:oc + 256].rearrange("p t (h c) -> p t h c", h=4)
                    step(nc.vector.tensor_tensor(o, o_in.rearrange("p (t h) c -> p t h c", t=NT),
                                                 rd.rearrange("p (t h) -> p t h", t=NT).unsqueeze(3)
                                                 .broadcast_to([P, NT, 4, HD]), ALU.mult), ("norm", e))
                    return
                g, br = int(pair[1]), 1 if pair[0] == "S" else 2
                rt = rd.rearrange("p (t h) -> p t h", t=NT)
                step(nc.vector.tensor_tensor(rt, rt, cgt3[:, :, 4 * g:4 * g + 4, br], ALU.mult))
                own(l)
                step(nc.vector.tensor_tensor(comb[:, :, :], o_in, rd.unsqueeze(2).broadcast_to([P, 8, HD]),
                                             ALU.mult))
                own(l)
                o = pr[:, :, oc:oc + 256]
                step(nc.vector.tensor_tensor(o, o, comb[:, :, :].rearrange("p (t h) c -> p t (h c)", t=NT),
                                             ALU.add), ("norm", e))

            def index_scores(l):
                dve.wait_ge(exp_done, l * len(PAIRS) + 1)
                for t in range(NT):
                    wv = work[:, 0:P] if t == 0 else work[:, P:3 * P]
                    for h in range(4):
                        own(l)
                        step(nc.vector.scalar_tensor_tensor(
                            wv, prob_view(0, t)[:, h, :], pr[:, t, I_W + h:I_W + h + 1],
                            cmask[:, t, 0:(t + 1) * P] if h == 0 else wv, ALU.mult, ALU.add), ("index",))

            def select_round(l, n):
                t = n // 8
                wv = work[:, 0:P] if t == 0 else work[:, P:3 * P]
                own(l)
                apart(dve)
                step(nc.vector.max(top8[:, :], wv))
                own(l)
                apart(dve)
                step(nc.vector.match_replace(wv, top8[:, :], wv, TAKEN))
                if n == 15:
                    own(l)
                    step(nc.vector.tensor_scalar(sel_b[:, :], work[:, :], TAKEN, -BIG, ALU.not_equal, ALU.mult),
                         ("selected",))

            def branch_out(l, br, order):
                for g in range(4):
                    half, t = g // 2, g % 2
                    if g < 3:
                        dve.wait_ge(y_ps, l * 9 + order * 3 + g + 1)
                    else:
                        wait_used(dve, l, FFN_SLABS + (M_BR, M_BR + 2, M_BR + 3)[order])
                    dve.wait_ge(gate_ready, l * 12 + 4 * br + 2 * half + t + 1)
                    gv = gate[:, t, br, half * 512:(half + 1) * 512]
                    bank = g + (4 if order == 1 else 0)
                    step(nc.vector.tensor_tensor(gv, ps[:, bank, :], gv, ALU.mult), ("gated", br, g))
                    if order == 2:
                        own(l)
                        dve.wait_ge(zsum, l * 4 + g + 1)
                        step(nc.vector.tensor_tensor(gv, gv, gate[:, t, 1, half * 512:(half + 1) * 512],
                                                     ALU.add), ("z", g))

            def turned_rest(l, n):
                k, bank = 2 * (n % 4), 4 + n % 4
                dve.wait_ge(ot_h, l * 8 + n + 1)
                step(nc.vector.tensor_tensor(ht_lo[:, k:k + 2, :].rearrange("p k c -> p (k c)"), ps[:, bank, :],
                                             ht_hi[:, k:k + 2, :].rearrange("p k c -> p (k c)").bitcast(F32),
                                             ALU.subtract), ("turned", n))

            def mixer(l):
                S = FFN_SLABS
                prep(l, 1, (2, 3))
                own(l) if count[0] else None
                step(nc.vector.memset(cmpm[:, :, :, :], 0.0), ("cmpm zero",))
                for m in range(11):
                    convert(l, S + m + 2, LASTU * 8 if m + 2 == 10 else SLAB)
                    if m % 2:
                        rope(l, m // 2)
                rope(l, 5)
                dve.wait_ge(cg_done, l + 1)
                step(nc.vector.tensor_scalar(cgt[:, :, :], cgt[:, :, :], 0.5, 0.5, ALU.mult, ALU.add))
                own(l)
                step(nc.vector.tensor_tensor(cgt3[:, :, :, 0], cgt3[:, :, :, 0],
                                             valid[:, :].unsqueeze(2).broadcast_to([P, NT, 8]), ALU.mult))
                for f in range(1, NFILL, 2):
                    fill_out(l, f)
                cmp_windows(l)
                convert(l, S + 15)
                compress(l)
                convert(l, S + 16)
                compressed_out(l)
                rounds = [0, 2, 3, 3, 3, 3, 2, 0, 0, 0]
                done = 0
                for e in range(NPOS):
                    if 1 <= e - 2:
                        normed(l, e - 2)
                    if 2 <= e - 1 < len(PAIRS):
                        dve.wait_ge(pt_ps, l * PT_LAYER + fills_before(e - 1) + 2)
                        dve.wait_ge(o_ps, l * 7 + e - 2)
                        step(nc.vector.tensor_copy(p_t[:, 1, :], ps[:, 6, :]), ("pt", e - 1))
                    if 0 < e < len(PAIRS):
                        maxima(l, e)
                    if e == 1:
                        index_scores(l)
                    convert(l, S + 17 + e)
                    for _ in range(rounds[e]):
                        select_round(l, done)
                        done += 1
                assert done == 16
                for n in range(4):
                    turned_rest(l, n)
                convert(l, S + 27)
                branch_out(l, 1, 0)
                convert(l, S + 28)
                convert(l, S + 29)
                convert(l, S + 30)
                branch_out(l, 2, 1)
                branch_out(l, 0, 2)
                for n in range(4, 8):
                    turned_rest(l, n)
                for m in range(31, 35):
                    convert(l, S + m)
                residual(l, 1, 0, 1.0, S + 32)

            dve.sem_inc(lo_done, 3)
            dve.wait_ge(x_loaded, 16)
            dve.sem_inc(x_new, 4)
            dve.wait_ge(setup_pe, 1)
            nc.vector.tensor_copy(cols[:, :], ps[:, 0, 0:112]).then_inc(setup_v, 1)
            dve.wait_ge(small_in, SMALL_DMAS * 16)
            dve.wait_ge(setup_g, SETUP_G)
            convert(0, 0)
            convert(0, 1)
            with dve.Fori(0, DEPTH) as l:
                ffn(l, 0)
                mixer(l)
                ffn(l, 1)
            assert count[0] == V_STEPS, count[0]
            gf = gr[:, 0:D]
            dve.wait_ge(setup_w, 16)
            for t in range(NT):
                dve.wait_ge(rstd_ready, (3 * DEPTH + 1) * 3)
                nc.vector.scalar_tensor_tensor(x[:, t, :], x[:, t, :], rstd[:, t:t + 1], gf, ALU.mult,
                                               ALU.mult).then_inc(x_new, 1)

        @block.gpsimd
        def _(pool):
            n = [0]

            def step(ins):
                n[0] += 1
                ins.then_inc(setup_g, 1)

            def own():
                pool.wait_ge(setup_g, n[0])

            step(nc.gpsimd.memset(ident[:, :], 0.0))
            step(nc.gpsimd.memset(ident_b[:, :], 0.0))
            own()
            for m in (ident, ident_b):
                step(nc.gpsimd.affine_select(out=m[:, :], in_=m[:, :], compare_op=ALU.not_equal, fill=1.0, base=0,
                                             pattern=[[-1, P]], channel_multiplier=1))
            step(nc.gpsimd.memset(cmask[:, :, :], 0.0))
            step(nc.gpsimd.memset(cmask_b[:, :, :], 0.0))
            step(nc.gpsimd.memset(kmask_b[:, :, :], 0.0))
            step(nc.gpsimd.memset(valid[:, :], 1.0))
            step(nc.gpsimd.memset(hsel[:, :], 1.0))
            step(nc.gpsimd.memset(mhalf[:, :], -0.5))
            step(nc.gpsimd.memset(kc_t[:, :, :, :], 0.0))
            step(nc.gpsimd.memset(k_t[:, :, :, :], 0.0))
            own()
            for m, fill in ((cmask, FILL), (cmask_b, -BIG)):
                step(nc.gpsimd.affine_select(out=m[:, :, :], in_=m[:, :, :], compare_op=ALU.is_ge, fill=fill, base=0,
                                             pattern=[[P, NT], [-1, SEQ]], channel_multiplier=1))
            step(nc.gpsimd.affine_select(out=kmask_b[:, :, :], in_=kmask_b[:, :, :], compare_op=ALU.is_ge, fill=-BIG,
                                         base=1 - CMP_BLOCK, pattern=[[P, NT], [-CMP_STRIDE, CPAD]],
                                         channel_multiplier=1))
            step(nc.gpsimd.affine_select(out=valid[:, :], in_=valid[:, :], compare_op=ALU.is_ge, fill=0.0,
                                         base=1 - CMP_BLOCK, pattern=[[P, NT]], channel_multiplier=1))
            step(nc.gpsimd.affine_select(out=hsel[:, :], in_=hsel[:, :], compare_op=ALU.is_ge, fill=0.0,
                                         base=0, pattern=[[-CPAD, 8]], channel_multiplier=1))
            own()
            step(nc.gpsimd.affine_select(out=hsel[:, :], in_=hsel[:, :], compare_op=ALU.is_ge, fill=0.0,
                                         base=CPAD - 1, pattern=[[CPAD, 8]], channel_multiplier=-1))
            assert n[0] == SETUP_G, n[0]
            pool.wait_ge(setup_v, 1)
            pool.wait_ge(small_in, SMALL_DMAS * 16)

            def layer_constants(l):
                nc.gpsimd.tensor_copy(gains.rearrange("p (n k) -> p n k", n=3),
                                      cols[:, 0:48].rearrange("p (n c) -> p n c", n=3)[:, :, ds(l * KD, KD)])\
                    .then_inc(cur_ready, 1)
                nc.gpsimd.tensor_copy(pos_c, cols[:, 48:112].rearrange("p (v c) -> p v c", v=2)[:, :, ds(l * 16, 16)])\
                    .then_inc(cur_ready, 1)
                nc.gpsimd.tensor_copy(cur[:, 3 * KD + 32:].unsqueeze(1),
                                      w2_all[:, ds(l, 1), :, :].rearrange("p a b c -> p a (b c)"))\
                    .then_inc(cur_ready, 1)

            def norm(p):
                pool.wait_ge(ssq_done, p * NT + NT)
                apart(pool)
                nc.gpsimd.tensor_scalar(msq[:, :], ssq[:, :], 1.0 / D, EPS, ALU.mult, ALU.add).then_inc(rstd_ready, 1)
                pool.wait_ge(rstd_ready, p * 3 + 1)
                nc.gpsimd.tensor_tensor(rstd[:, :], msq[:, :], mhalf[:, :], ALU.pow).then_inc(rstd_ready, 1)
                pool.wait_ge(rstd_ready, p * 3 + 2)
                apart(pool)
                nc.gpsimd.tensor_scalar(hrstd[:, :], rstd[:, :], 0.5, None, ALU.mult).then_inc(rstd_ready, 1)

            with pool.Fori(0, DEPTH) as l:
                pool.wait_ge(x_new, l * 12 + 1)
                layer_constants(l)
                norm(l * 3)
                norm(l * 3 + 1)
                for w in range(6):
                    for t in range(NT):
                        pool.wait_ge(gate_t, l * 12 + 2 * w + t + 1)
                        apart(pool)
                        gv = gate[:, t, w // 2, (w % 2) * 512:(w % 2 + 1) * 512]
                        nc.gpsimd.tensor_scalar(gv, gv, 0.5, 0.5, ALU.mult, ALU.add).then_inc(gate_ready, 1)
                for g in range(4):
                    half, t = g // 2, g % 2
                    wait_step(pool, l, ("gated", 2, g))
                    a, b = (gate[:, t, br, half * 512:(half + 1) * 512] for br in (1, 2))
                    nc.gpsimd.tensor_tensor(a, a, b, ALU.add).then_inc(zsum, 1)
                norm(l * 3 + 2)
            norm(3 * DEPTH)

        @block.scalar
        def _(eng):
            for dst, src in small_loads():
                eng.dma_start(dst, src).then_inc(small_in, 16)

            def convert(l, s, w=SLAB):
                wait_raw(eng, l, s)
                i, c = of(s)
                wait_used(eng, l, (i, c - 3))
                n = slot(s)
                nc.scalar.activation(whi[:, n, 0:w], raw[:, n, 0:w], ACT.Copy).then_inc(hi_done, 1)

            def squares(p):
                for t in range(NT):
                    nc.scalar.activation(p_t[:, t, :].bitcast(BF16), x[:, t, :], ACT.Square,
                                         accum_out=ssq[:, t:t + 1]).then_inc(ssq_done, 1)

            def prep(l, n, banks):
                for k in range(KD):
                    eng.wait_ge(xt_ps, (l * 3 + n) * 4 + k // 2 + 1)
                    src = ps[:, banks[(k // 2) % 2], (k % 2) * SEQ:(k % 2 + 1) * SEQ]
                    nc.scalar.activation(ht_hi[:, k, :], src, ACT.Copy,
                                         scale=gains[:, n * KD + k:n * KD + k + 1]).then_inc(hth, 1)
                squares(l * 3 + n)

            def silu(l, f, i, first):
                r, s0 = l * 2 + f, f * (FFN_SLABS + MIX_SLABS)
                wait_used(eng, l, s0 + 1 if first else (i, s0))
                for t in range(NT):
                    if not first:
                        eng.wait_ge(act_done, r * (2 * NSTEP) + i * 2 + t - 1)
                    nc.scalar.activation(sg[:, t, :], ps[:, t, 0:FSTEP], ACT.Silu,
                                         scale=rstd[:, t:t + 1]).then_inc(silu_done, 1)

            def act_round(l, f, i):
                eng.wait_ge(at_ps, (l * 2 + f) * NSTEP + i + 1)
                nc.scalar.activation(at_hi[:, :, :].rearrange("p j c -> p (j c)"), ps[:, 2, :],
                                     ACT.Copy).then_inc(ath, 1)

            def ffn(l, f):
                n, s0 = 2 * f, f * (FFN_SLABS + MIX_SLABS)
                if f == 0:
                    eng.wait_ge(cur_ready, l * 3 + 3)
                prep(l, n, (2, 3) if f == 0 else (4, 5))
                convert(l, s0 + 2)
                eng.wait_ge(rstd_ready, (l * 3 + n) * 3 + 3)
                silu(l, f, 0, True)
                convert(l, s0 + 3)
                act_round(l, f, 0)
                with eng.Fori(1, NSTEP) as i:
                    convert(l, (i, s0 + 1))
                    convert(l, (i, s0 + 2))
                    silu(l, f, i, False)
                    convert(l, (i, s0 + 3))
                    act_round(l, f, i)
                convert(l, s0 + FFN_SLABS + 1)

            def project_out(l, u):
                w = 512 if u < 5 else LASTU
                wait_used(eng, l, FFN_SLABS + (2 * u + 1 if u < 5 else 10))
                for t in range(NT):
                    nc.scalar.activation(pr[:, t, u * 512:u * 512 + w], ps[:, 2 * (u % 2) + t, 0:w], ACT.Copy,
                                         scale=rstd[:, t:t + 1]).then_inc(proj_done, 1)

            def gates(l, w):
                wait_used(eng, l, FFN_SLABS + (12 if w == 0 else 16 + 2 * (w - 1)))
                for t in range(NT):
                    nc.scalar.activation(gate[:, t, w // 2, (w % 2) * 512:(w % 2 + 1) * 512], ps[:, t, :], ACT.Tanh,
                                         scale=hrstd[:, t:t + 1]).then_inc(gate_t, 1)

            def exps(l, e):
                pair, b = PAIRS[e], e % 2
                if pair == "I":
                    for t in range(NT):
                        eng.wait_ge(sc_ps, l * 16 + 2 * e + t + 1)
                        ins = nc.scalar.activation(prob_view(b, t), score_views(t), ACT.Relu, scale=IDX_SCALE)
                    ins.then_inc(exp_done, 1)
                    return
                wait_step(eng, l, ("max", e))
                if pair == "C":
                    pv = prob[:, b, 0:256]
                    nc.scalar.activation(pv, pv, ACT.Exp).then_inc(exp_done, 1)
                    return
                if e == 2:
                    wait_step(eng, l, ("index",))
                for t in range(NT):
                    for h in range(4):
                        ins = nc.scalar.activation(prob_view(b, t)[:, h, :], score_views(t)[:, h, :], ACT.Exp,
                                                   bias=nmax[:, b, 4 * t + h:4 * t + h + 1],
                                                   accum_out=den[:, b, 4 * t + h:4 * t + h + 1])
                ins.then_inc(exp_done, 1)

            def prob_out(l, e, f):
                eng.wait_ge(pt_ps, l * PT_LAYER + fills_before(e) + f + 1)
                if e > 1:
                    eng.wait_ge(o_ps, l * 7 + e - 1)
                w = 256 if PAIRS[e] == "C" else 512
                nc.scalar.activation(p_t[:, f, 0:w], ps[:, 5, 0:w], ACT.Copy).then_inc(pt_a, 1)

            def turned(l, n):
                k, bank = 2 * (n % 4), 4 + n % 4
                eng.wait_ge(ot_ps, l * 8 + n + 1)
                nc.scalar.activation(ht_hi[:, k:k + 2, :].rearrange("p k c -> p (k c)"), ps[:, bank, :],
                                     ACT.Copy).then_inc(ot_h, 1)

            def mixer(l):
                S = FFN_SLABS
                prep(l, 1, (2, 3))
                eng.wait_ge(rstd_ready, (l * 3 + 1) * 3 + 3)
                for m in range(11):
                    convert(l, S + m + 2, LASTU * 8 if m + 2 == 10 else SLAB)
                    if m % 2:
                        project_out(l, m // 2)
                project_out(l, 5)
                eng.wait_ge(proj_done, l * 12 + 12)
                nc.scalar.activation(cgt[:, :, :], pr[:, :, C_G:C_G + 24], ACT.Tanh, scale=0.5).then_inc(cg_done, 1)
                for f in range(0, NFILL, 2):
                    eng.wait_ge(fill_ps, l * NFILL + f + 1)
                    copy_fill(lambda o, i, k: copied.append(nc.scalar.activation(o, i, ACT.Copy, scale=k)), f)
                    copied.pop().then_inc(fill_a, 1)
                    copied.clear()
                gates(l, 0)
                convert(l, S + 15)
                wait_step(eng, l, ("gelu arg",))
                nc.scalar.activation(hid3[:, :], hid2[:, :], ACT.Tanh, scale=0.7978845608028654).then_inc(gelu_t, 1)
                convert(l, S + 16)
                for e in range(NPOS):
                    if e in (2, 4, 6, 8):
                        gates(l, e // 2)
                    if 1 <= e - 1 < len(PAIRS):
                        prob_out(l, e - 1, 0)
                    convert(l, S + 17 + e)
                    if 2 <= e - 1 < len(PAIRS):
                        prob_out(l, e - 1, 2)
                    if e < len(PAIRS):
                        exps(l, e)
                gates(l, 5)
                for n in range(4):
                    turned(l, n)
                for m in range(27, 31):
                    convert(l, S + m)
                for n in range(4, 8):
                    turned(l, n)
                for m in range(31, 35):
                    convert(l, S + m)

            copied = []
            convert(0, 0)
            convert(0, 1)
            with eng.Fori(0, DEPTH) as l:
                ffn(l, 0)
                mixer(l)
                ffn(l, 1)
            eng.wait_ge(x_new, 3 * DEPTH * 4 + 4)
            squares(3 * DEPTH)

        @block.tensor
        def _(pe):
            def three(o, xh, xl, wh, wl, start, stop):
                nc.tensor.matmul(o, xh, wh, start=start, stop=False)
                nc.tensor.matmul(o, xh, wl, start=False, stop=False)
                return nc.tensor.matmul(o, xl, wh, start=False, stop=stop)

            def ready(l, s):
                wait_hi(pe, l, s)
                wait_lo(pe, l, s)

            def prep(l, n, banks):
                for b in range(4):
                    pe.wait_ge(x_new, (l * 3 + n) * 4 + 2 * (b // 2) + 2)
                    if b >= 2:
                        pe.wait_ge(htl, (l * 3 + n) * KD + 2 * (b - 1))
                    for j in range(2):
                        for t in range(NT):
                            ins = nc.tensor.transpose(ps[:, banks[b % 2], j * SEQ + t * P:j * SEQ + (t + 1) * P],
                                                      x[:, t, (2 * b + j) * P:(2 * b + j + 1) * P], ident[:, :])
                    ins.then_inc(xt_ps, 1)

            def wide(l, s, k0, nk, banks, width, kstart, kstop, first=False, n=0):
                ready(l, s)
                wv = whi[:, slot(s), 0:nk * width].rearrange("p (k c) -> p k c", k=nk)
                wr = wlo[:, slot(s), 0:nk * width].rearrange("p (k c) -> p k c", k=nk)
                for kk in range(nk):
                    k = k0 + kk
                    if first:
                        pe.wait_ge(htl, (l * 3 + n) * KD + k + 1)
                    for t in range(NT):
                        ins = three(ps[:, banks[t], 0:width], ht_hi[:, k, t * P:(t + 1) * P],
                                    ht_lo[:, k, t * P:(t + 1) * P], wv[:, kk, :], wr[:, kk, :],
                                    k == kstart, k == kstop)
                ins.then_inc(slab_used, 1)

            def tall(l, s, hi, lo, k0, bank0, start, stop, signal=None):
                ready(l, s)
                wv = whi[:, slot(s), :].rearrange("p (j c) -> p j c", j=2)
                wr = wlo[:, slot(s), :].rearrange("p (j c) -> p j c", j=2)
                for g in range(4):
                    half, t = g // 2, g % 2
                    for j in range(2):
                        ins = three(ps[:, bank0 + g, :], hi[:, k0 + j, t * P:(t + 1) * P],
                                    lo[:, k0 + j, t * P:(t + 1) * P], wv[:, j, half * 512:(half + 1) * 512],
                                    wr[:, j, half * 512:(half + 1) * 512], start and j == 0, stop and j == 1)
                    if g == 3:
                        ins.then_inc(slab_used, 1)
                    elif signal is not None:
                        ins.then_inc(signal, 1)

            def gate_up(l, f, i, first=False):
                r, s0 = l * 2 + f, f * (FFN_SLABS + MIX_SLABS)
                if not first:
                    pe.wait_ge(act_done, r * (2 * NSTEP) + i * 2)
                for a in range(2):
                    s = s0 + a if first else (i, s0 - 1 + a)
                    wide(l, s, 4 * a, 4, (0, 1), 512, 0, KD - 1, first, 2 * f)

            def turn(l, f, i):
                r = l * 2 + f
                pe.wait_ge(act_done, r * (2 * NSTEP) + i * 2 + 2)
                for j in range(2):
                    for t in range(NT):
                        ins = nc.tensor.transpose(ps[:, 2, j * SEQ + t * P:j * SEQ + (t + 1) * P],
                                                  act[:, t, j * P:(j + 1) * P], ident[:, :])
                ins.then_inc(at_ps, 1)

            def down(l, f, i, s, start=False, stop=False, signal=None):
                pe.wait_ge(atl, (l * 2 + f) * NSTEP + i + 1)
                tall(l, s, at_hi, at_lo, 0, 4, start, stop, signal)

            def ffn(l, f):
                s0 = f * (FFN_SLABS + MIX_SLABS)
                prep(l, 2 * f, (2, 3) if f == 0 else (4, 5))
                gate_up(l, f, 0, True)
                turn(l, f, 0)
                gate_up(l, f, 1)
                down(l, f, 0, s0 + 4, start=True)
                turn(l, f, 1)
                with pe.Fori(2, NSTEP) as i:
                    gate_up(l, f, i)
                    down(l, f, i - 1, (i, s0 + 1))
                    turn(l, f, i)
                down(l, f, NSTEP - 1, s0 + FFN_SLABS - 1, stop=True, signal=sub_out)

            def fill(l, f):
                bank = 4 + f % 4
                if f >= 4:
                    if f % 2:
                        wait_step(pe, l, ("fill", f - 4))
                    else:
                        pe.wait_ge(fill_a, l * 7 + (f - 4) // 2 + 1)
                for j in range(2):
                    for t in range(NT):
                        cols_out = slice(j * SEQ + t * P, j * SEQ + (t + 1) * P)
                        if f < len(FILLS):
                            b = FILLS[f][0][j]
                            src = rs[:, t, b, :] if b < NRB else \
                                pr[:, t, C_Q + (b - NRB) * P:C_Q + (b - NRB + 1) * P]
                            ins = nc.tensor.transpose(ps[:, bank, cols_out], src, ident[:, :])
                        else:
                            c0 = (C_KC if f == len(FILLS) else C_VC) + j * HD
                            for p0 in (0, HD):
                                ins = nc.tensor.matmul(ps[p0:p0 + HD, bank, cols_out], pr[:, t, c0:c0 + HD],
                                                       ident[:, :], start=True, stop=True)
                ins.then_inc(fill_ps, 1)

            def compress(l, v):
                s = FFN_SLABS + M_CK + v
                wait_raw(pe, l, s)
                w1 = raw[:, slot(s), :].rearrange("p (j c) -> p j c", j=16)
                for j in range(16):
                    ins = nc.tensor.matmul(ps[:, 7, 32 * v:32 * v + 32], w1[:, j, :], cmpm[:, v, j, :],
                                           start=j == 0, stop=j == 15)
                ins.then_inc(slab_used, 1)

            def scores(l, e):
                pair = PAIRS[e]
                if e:
                    pe.wait_ge(exp_done, l * len(PAIRS) + e)
                qb, kb, kstep, _, _ = heads_of(pair) if pair != "C" else (0,) * 5
                if pair == "A":
                    wait_step(pe, l, ("selected",))
                for t in range(NT):
                    if pair == "C":
                        nc.tensor.matmul(ps[:, 4, t * P:(t + 1) * P], ident_b[:, :],
                                         kmask_b[:, t, :].unsqueeze(1).broadcast_to([P, 8, CPAD]),
                                         start=t == 0, stop=False, skip_group_check=True)
                        for j in range(4):
                            ins = nc.tensor.matmul(ps[:, 4, t * P + 32 * j:t * P + 32 * j + 32],
                                                   qn_t[:, j, t * P:(t + 1) * P],
                                                   kc_t[:, j // 2, :, :].rearrange("p a c -> p (a c)"),
                                                   start=False, stop=t == 1 and j == 3, skip_group_check=True)
                        ins.then_inc(sc_ps, 1)
                        continue
                    nk = (t + 1) * P
                    for b in range(t + 1):
                        bank = 4 if t == 0 else 2 + b
                        nh = 512 // nk
                        opened = False
                        masks = [] if pair == "I" else [cmask_b[:, t, 0:nk]]
                        if pair == "A":
                            masks.append(sel_b[:, 0:P] if t == 0 else sel_b[:, P:3 * P])
                        for mk in masks:
                            nc.tensor.matmul(ps[:, bank, :], ident_b[:, :],
                                             mk.unsqueeze(1).broadcast_to([P, nh, nk]),
                                             start=not opened, stop=False, skip_group_check=True)
                            opened = True
                        for j in range(nh // 2):
                            jj = b + j if t == 1 else j
                            ins = nc.tensor.matmul(ps[:, bank, j * 2 * nk:(j + 1) * 2 * nk],
                                                   q_t[:, qb + jj, t * P:(t + 1) * P],
                                                   k_t[:, kb + kstep * jj, :, 0:nk],
                                                   start=not opened, stop=j == nh // 2 - 1,
                                                   skip_group_check=True)
                            opened = True
                    ins.then_inc(sc_ps, 1)

            def turn_probs(l, e, f):
                pair, b = PAIRS[e], e % 2
                if f == 0:
                    pe.wait_ge(exp_done, l * len(PAIRS) + e + 1)
                if pair == "C":
                    for t in range(NT):
                        ins = nc.tensor.transpose(ps[:, 5, t * P:(t + 1) * P], prob[:, b, t * P:(t + 1) * P],
                                                  ident[:, :])
                    ins.then_inc(pt_ps, 1)
                    return
                if f == 1 and PAIRS[e - 1] == "C":
                    wait_step(pe, l, ("norm", e - 1))
                if f == 2:
                    pe.wait_ge(pt_a, l * PT_ACT + acts_before(e) + 1)
                t, kt = PT_FILLS[f]
                for h in range(4):
                    ins = nc.tensor.transpose(ps[:, 6 if f == 1 else 5, h * P:(h + 1) * P],
                                              prob_view(b, t)[:, h, kt * P:(kt + 1) * P], ident[:, :])
                ins.then_inc(pt_ps, 1)

            def weighted(l, e):
                pair = PAIRS[e]
                pe.wait_ge(pt_a, l * PT_ACT + acts_before(e + 1))
                if e > 1:
                    wait_step(pe, l, ("pt", e))
                    wait_step(pe, l, ("norm", e - 1))
                if pair == "C":
                    for t in range(NT):
                        ins = nc.tensor.matmul(ps[:, 7 - t, :], p_t[:, 0, t * P:(t + 1) * P],
                                               v_blk[:, :, :].rearrange("p h c -> p (h c)"), start=True, stop=True)
                    ins.then_inc(o_ps, 1)
                    return
                vcol = heads_of(pair)[3]
                for t in range(NT):
                    for h in range(4):
                        for f, (ft, kt) in enumerate(PT_FILLS):
                            if ft != t:
                                continue
                            ins = nc.tensor.matmul(ps[:, 7, (t * 4 + h) * HD:(t * 4 + h + 1) * HD],
                                                   p_t[:, f, h * P:(h + 1) * P],
                                                   pr[:, kt, vcol(h):vcol(h) + HD], start=kt == 0, stop=kt == t,
                                                   skip_group_check=True)
                ins.then_inc(o_ps, 1)

            def turn_out(l, n):
                for j in range(2):
                    for t in range(NT):
                        k = 2 * (n % 4) + j
                        if n < 4:
                            c0 = (B_Q + k * P) if k < 2 else (C_Q + (k - 2) * P) if k < 6 else (A_Q + (k - 6) * P)
                            src = pr[:, t, c0:c0 + P]
                        else:
                            src = gate[:, t, 0, k * P:(k + 1) * P]
                        ins = nc.tensor.transpose(ps[:, 4 + n % 4, j * SEQ + t * P:j * SEQ + (t + 1) * P], src,
                                                  ident[:, :])
                ins.then_inc(ot_ps, 1)

            def mixer(l):
                S = FFN_SLABS
                prep(l, 1, (2, 3))
                for u in range(5):
                    banks = (2 * (u % 2), 2 * (u % 2) + 1)
                    if u >= 2:
                        pe.wait_ge(proj_done, l * 12 + 2 * (u - 1))
                    for a in range(2):
                        wide(l, S + 2 * u + a, 4 * a, 4, banks, 512, 0, KD - 1, u == 0, 1)
                pe.wait_ge(proj_done, l * 12 + 8)
                wide(l, S + 10, 0, KD, (2, 3), LASTU, 0, KD - 1)
                wait_step(pe, l, ("rope", 3))
                for f in range(T1):
                    if f == 0:
                        pe.wait_ge(proj_done, l * 12 + 10)
                    fill(l, f)
                wide(l, S + 11, 0, 4, (0, 1), 512, 0, KD - 1)
                pe.wait_ge(proj_done, l * 12 + 12)
                wait_step(pe, l, ("rope", 5))
                for f in range(T1, NFILL):
                    fill(l, f)
                wide(l, S + 12, 4, 4, (0, 1), 512, 0, KD - 1)
                wait_step(pe, l, ("windows",))
                compress(l, 0)
                compress(l, 1)
                wait_step(pe, l, ("hidden",))
                nc.tensor.matmul(ps[:, 7, 64:96], w2k, hid[:, 0:32], start=True, stop=True).then_inc(cmp_ps, 1)
                nc.tensor.matmul(ps[:, 7, 96:160], hid_v[:, :, :].rearrange("p h c -> p (h c)"), w2v, start=True,
                                 stop=True).then_inc(cmp_ps, 1)
                wait_step(pe, l, ("fill", 9))
                pe.wait_ge(fill_a, l * 7 + 7)
                for e in range(NPOS):
                    if e == 1:
                        wait_step(pe, l, ("v_blk",))
                    if 1 <= e - 1 < len(PAIRS):
                        turn_probs(l, e - 1, 0)
                        if e - 1 > 1:
                            turn_probs(l, e - 1, 1)
                    if e < len(PAIRS):
                        scores(l, e)
                    if 2 <= e - 1 < len(PAIRS):
                        turn_probs(l, e - 1, 2)
                    if e % 2 == 0:
                        pe.wait_ge(gate_t, l * 12 + e + 2)
                    wide(l, S + 15 + e, 4 * (e % 2), 4, (0, 1), 512, 0, KD - 1)
                    if 1 <= e - 1 < len(PAIRS):
                        weighted(l, e - 1)
                wait_step(pe, l, ("norm", len(PAIRS) - 1))
                for n in range(4):
                    turn_out(l, n)
                pe.wait_ge(gate_t, l * 12 + 12)
                wait_step(pe, l, ("turned", 0))
                tall(l, S + 25, ht_hi, ht_lo, 0, 0, True, True, y_ps)
                wait_step(pe, l, ("turned", 3))
                tall(l, S + 26, ht_hi, ht_lo, 2, 4, True, False)
                tall(l, S + 27, ht_hi, ht_lo, 4, 4, False, True, y_ps)
                wait_step(pe, l, ("gated", 1, 3))
                tall(l, S + 28, ht_hi, ht_lo, 6, 0, True, True, y_ps)
                for n in range(4, 8):
                    wait_step(pe, l, ("z", 1 if n < 6 else 3))
                    turn_out(l, n)
                for a in range(4):
                    wait_step(pe, l, ("turned", 4 + a))
                    tall(l, S + 29 + a, ht_hi, ht_lo, 2 * a, 0, a == 0, a == 3, sub_out if a == 3 else None)

            pe.sem_inc(slab_used, 3)
            pe.wait_ge(small_in, SMALL_DMAS * 16)
            pe.wait_ge(setup_g, SETUP_G)
            nc.tensor.transpose(ps[:, 0, 0:112], rows[:, :], ident[0:112, 0:112]).then_inc(setup_pe, 1)
            with pe.Fori(0, DEPTH) as l:
                ffn(l, 0)
                mixer(l)
                ffn(l, 1)

        @block.sync
        def _(sp):
            def load(l, s, parts):
                i, c = of(s)
                before = c - 3
                if before in (S_CK, S_CV):
                    wait_used(sp, l, before)
                else:
                    b = splits(before) if before >= 0 else before
                    sp.wait_ge(lo_done, l * LAYER_SPLITS + i * 3 + b + 1 + 3)
                for dst, src in parts:
                    sp.dma_start(dst, src).then_inc(raw_in[slot(s)], 16)

            def rows_cols(w, l, r0, nk, c0, n):
                v = w[ds(l, 1), ds(r0, nk * P), ds(c0, n)]
                return v.rearrange("a (k p) c -> p (a k) c", p=P)

            def slab(s, nk):
                return lambda w: raw[:, slot(s), 0:nk * w].rearrange("p (k c) -> p k c", k=nk)

            def load_gate_up(l, s, wg, wu, a, col):
                v = slab(s, 4)(512)
                load(l, s, [(v[:, :, 0:FSTEP], rows_cols(wg, l, 512 * a, 4, col, FSTEP)),
                            (v[:, :, FSTEP:], rows_cols(wu, l, 512 * a, 4, col, FSTEP))])

            def load_halves(l, s, w, r0, nk, c0, n):
                v = slab(s, nk)(n)
                h = nk // 2
                load(l, s, [(v[:, 0:h, :], rows_cols(w, l, r0, h, c0, n)),
                            (v[:, h:nk, :], rows_cols(w, l, r0 + h * P, h, c0, n))])

            def ffn(l, f, wg, wu, wd):
                s0 = f * (FFN_SLABS + MIX_SLABS)
                for a in range(2):
                    load_gate_up(l, s0 + a, wg, wu, a, 0)
                with sp.Fori(1, NSTEP) as i:
                    for a in range(2):
                        load_gate_up(l, (i, s0 - 1 + a), wg, wu, a, i * FSTEP)
                    load_halves(l, (i, s0 + 1), wd, i * FSTEP - FSTEP, 2, 0, D)
                load_halves(l, s0 + FFN_SLABS - 1, wd, DFF - FSTEP, 2, 0, D)

            def mixer(l):
                S = FFN_SLABS
                for m in range(10):
                    load_halves(l, S + m, w_in, 512 * (m % 2), 4, 512 * (m // 2), 512)
                load_halves(l, S + 10, w_in, 0, 8, 5 * 512, LASTU)
                for m in (11, 12):
                    load_halves(l, S + m, w_in, 512 * (m - 11), 4, M_G, 512)
                load_halves(l, S + M_CK, cmp_w1_k, 0, 16, 0, P)
                load_halves(l, S + M_CV, cmp_w1_v, 0, 16, 0, P)
                for q in range(2, 12):
                    load_halves(l, S + 13 + q, w_in, 512 * (q % 2), 4, M_G + 512 * (q // 2), 512)
                for m, w, r0 in ((25, w_branch_b, 0), (26, w_branch_c, 0), (27, w_branch_c, 256),
                                 (28, w_branch_a, 0), (29, w_out, 0), (30, w_out, 256), (31, w_out, 512),
                                 (32, w_out, 768)):
                    load_halves(l, S + m, w, r0, 2, 0, D)

            sp.dma_start(x[:, :, :], x_in.rearrange("a (t p) d -> p (a t) d", p=P)).then_inc(x_loaded, 16)
            with sp.Fori(0, DEPTH) as l:
                ffn(l, 0, ffn1_w_gate, ffn1_w_up, ffn1_w_down)
                mixer(l)
                ffn(l, 1, ffn2_w_gate, ffn2_w_up, ffn2_w_down)
            for a in range(2):
                v = slab(a, 4)(512)
                sp.wait_ge(lo_done, DEPTH * LAYER_SPLITS + a - 3 + 1 + 3)
                for part, w in ((v[:, :, 0:FSTEP], ffn1_w_gate), (v[:, :, FSTEP:], ffn1_w_up)):
                    sp.dma_start(part, w[0, 512 * a:512 * (a + 1), 0:FSTEP].rearrange("(k p) c -> p k c", p=P))\
                        .then_inc(raw_in[a], 16)
            sp.wait_ge(x_new, 3 * DEPTH * 4 + 1)
            sp.dma_start(gr[:, 0:D], final_norm.rearrange("(a d) -> a d", a=1).broadcast_to([P, D]))\
                .then_inc(setup_w, 16)
            sp.wait_ge(x_new, 3 * DEPTH * 4 + 4 + NT)
            sp.dma_start(out.rearrange("a (t p) d -> p (a t) d", p=P), x[:, :, :]).then_inc(out_done, 16)
            sp.wait_ge(out_done, 16)


_INS = ["x", "ffn1_norm", "ffn1_w_gate", "ffn1_w_up", "ffn1_w_down", "mix_norm", "w_in", "cmp_pos_k", "cmp_w1_k",
        "cmp_w2_k", "cmp_pos_v", "cmp_w1_v", "cmp_w2_v", "w_branch_a", "w_branch_b", "w_branch_c", "w_out",
        "ffn2_norm", "ffn2_w_gate", "ffn2_w_up", "ffn2_w_down", "final_norm"]


def rope_tables():
    half = HD // 2
    inv = np.float32(10000.0) ** (-np.arange(half, dtype=np.float32) / np.float32(half))
    ang = np.arange(SEQ, dtype=np.float32)[:, None] * inv[None, :].astype(np.float32)
    c, s = np.cos(ang).astype(np.float32), np.sin(ang).astype(np.float32)
    return np.concatenate([c, c], 1), np.concatenate([-s, s], 1)


def kernel(**inputs):
    import concourse.bacc as _bacc
    from concourse.bass_utils import run_bass_kernel_spmd as _run

    nc = _bacc.Bacc("TRN2", target_bir_lowering=False, num_devices=1)
    arrays, args = {}, []
    given = [(name, np.ascontiguousarray(inputs[name])) for name in _INS]
    given += list(zip(("cos_t", "sin_t"), rope_tables()))
    for name, a in given:
        arrays[f"in_{name}_dram"] = a
        args.append(nc.dram_tensor(f"in_{name}_dram", a.shape, mybir.dt.from_np(a.dtype), kind="ExternalInput").ap())
    args.append(nc.dram_tensor("out_0_dram", (1, SEQ, D), F32, kind="ExternalOutput").ap())
    build(nc, *args)
    r = _run(nc, [arrays], core_ids=[0])
    return r.results[0]["out_0_dram"]
```

```python
from contextlib import ExitStack

import numpy as np

import concourse.bass as bass
from concourse import mybir

F32 = mybir.dt.float32
F32R = mybir.dt.float32r
BF16 = mybir.dt.bfloat16
ALU = mybir.AluOpType
ACT = mybir.ActivationFunctionType
AX_X = mybir.AxisListType.X
ds = bass.ds

P = 128
SEQ, D, DFF, DEPTH = 256, 1024, 2816, 2
NT = SEQ // P
KD = D // P
HD = 64
EPS = 1e-6
ATT_SCALE = HD ** -0.5
IDX_SCALE = (4 * HD) ** -0.5
TOPK = SEQ // 4
NCMP, CMP_STRIDE, CMP_BLOCK = 15, 16, 32
CPAD = 16
BIG = 1e30
FILL = -3.0e38
TAKEN = -3.4e38

A_Q, A_K, A_V, I_Q, I_K, I_W = 0, 256, 320, 384, 640, 704
B_Q, B_K, B_V, C_Q = 708, 964, 1220, 1476
C_KC, C_VC, C_KS, C_VS, C_KW, C_VW, C_G, M_G = 1988, 2116, 2244, 2372, 2500, 2628, 2756, 2780
NPROJ = M_G
LASTU = NPROJ - 5 * 512

SLAB = 2048
FSTEP = 256
NSTEP = DFF // FSTEP
FFN_SLABS = 3 * NSTEP
MIX_SLABS = 33
LAYER_SLABS = 2 * FFN_SLABS + MIX_SLABS
M_CK, M_CV = 13, 14
S_CK, S_CV = FFN_SLABS + M_CK, FFN_SLABS + M_CV
LAYER_SPLITS = LAYER_SLABS - 2
M_BR, M_WO = 25, 29

QBLK = {"A": 0, "I": 2, "B": 4, "R": 6}
KBLK = {"A": 0, "I": 1, "B": 2, "S": 4, "W": 6}
NQB, NKB, NRB = 10, 8, 18
ROPE = {
    0: [(A_Q, 4, 0, False), (A_K, 1, 2, True)],
    1: [(I_Q, 4, 3, False), (I_K, 1, 5, True), (B_Q, 4, 6, False)],
    2: [(B_K, 4, 8, False)],
    3: [(C_Q, 8, 10, False)],
    4: [(C_KS, 2, 14, True)],
    5: [(C_KW, 2, 16, True)],
}
FILLS = [((0, 1), ("qs", 0), ("qs", 1)), ((2, 3), ("k", 0), ("q", 2)), ((4, 5), ("q", 3), ("k", 1)),
         ((6, 7), ("qs", 4), ("qs", 5)), ((8, 9), ("k", 2), ("k", 3)), ((10, 11), ("qs", 6), ("qs", 7)),
         ((12, 13), ("qs", 8), ("qs", 9)), ((14, 15), ("k", 4), ("k", 5)), ((16, 17), ("k", 6), ("k", 7)),
         ((18, 19), ("n", 0), ("n", 1)), ((20, 21), ("n", 2), ("n", 3))]
NFILL = len(FILLS) + 2
T1 = 5

PAIRS = ["I", "C", "B", "S0", "S1", "W0", "W1", "A"]
NPOS = len(PAIRS) + 2
V_STEPS = 185
SETUP_WARM, SETUP_G = 1, 17


def build(nc, x_in, ffn1_w_gate, ffn1_w_up, ffn1_w_down, w_in, cmp_w1_k, cmp_w2_k, cmp_w1_v, cmp_w2_v,
          w_branch_a, w_branch_b, w_branch_c, w_out, ffn2_w_gate, ffn2_w_up, ffn2_w_down, final_norm,
          rows_dram, cos_t, sin_t, out):
    ctx = ExitStack()
    with ctx:
        def sb(name, shape, dt=F32):
            return ctx.enter_context(nc.sbuf_tensor(name, shape, dt))

        def sem(name):
            return ctx.enter_context(nc.semaphore(name))

        raw = sb("raw", [P, 3, SLAB])
        whi = sb("whi", [P, 3, SLAB], F32R)
        wlo = sb("wlo", [P, 3, SLAB], F32R)
        x = sb("x", [P, NT, D])
        ht_hi = sb("ht_hi", [P, KD, SEQ], F32R)
        ht_lo = sb("ht_lo", [P, KD, SEQ], F32R)
        at_hi = sb("at_hi", [P, 2, SEQ], F32R)
        at_lo = sb("at_lo", [P, 2, SEQ], F32R)
        scr = sb("scr", [P, 4 * SEQ])
        sg = scr[:, 0:512].rearrange("p (t c) -> p t c", t=NT)
        act = scr[:, 512:1024].rearrange("p (t c) -> p t c", t=NT)
        kvs = scr[:, :].rearrange("p (v g c) -> p v g c", v=2, g=2)
        pr = sb("proj", [P, NT, NPROJ])
        gr = sb("gates", [P, NT * 3 * D])
        gate = gr[:, :].rearrange("p (t b c) -> p t b c", t=NT, b=3)
        rs = gr[:, 0:NT * NRB * P].rearrange("p (t b c) -> p t b c", t=NT, b=NRB)
        cmpm = gr[:, NT * NRB * P:NT * NRB * P + 1024].rearrange("p (v j c) -> p v j c", v=2, j=16)
        q_t = sb("q_t", [P, NQB, SEQ])
        k_t = sb("k_t", [P, NKB, 2, SEQ])
        prob = sb("prob", [P, 2, 1536])
        qn_t = prob[:, 1, 512:1536].rearrange("p (b c) -> p b c", b=4)
        p_t = sb("p_t", [P, 3, 512])
        hid_rows = p_t[0:2 * CPAD, 0, 0:2 * P]
        cos_s = sb("cos_s", [P, NT, HD])
        sin_s = sb("sin_s", [P, NT, HD])
        rtmp = prob[:, 0, 0:NT * 8 * HD].rearrange("p (t h c) -> p t h c", t=NT, h=8)
        last_ms = sb("last_ms", [P, 2 * NT])
        warm = sb("warm", [P, 1])
        ident = sb("ident", [P, P])
        ident_b = sb("ident_b", [P, P], BF16)
        cmask = sb("cmask", [P, NT, SEQ])
        cmask_b = sb("cmask_b", [P, NT, SEQ], BF16)
        kmask_b = sb("kmask_b", [P, NT, CPAD], BF16)
        valid = sb("valid", [P, NT])
        hsel = sb("hsel", [P, 8])
        rows = sb("rows", [112, P])
        cols = sb("cols", [P, 112])
        w2_all = sb("w2_all", [P, DEPTH, 3, HD])
        cur = sb("cur", [P, 3 * KD + 32 + 3 * HD])
        ssq = sb("ssq", [P, NT])
        msq = sb("msq", [P, NT])
        mhalf = sb("mhalf", [P, NT])
        rstd = sb("rstd", [P, NT])
        hrstd = sb("hrstd", [P, NT])
        work = sb("work", [P, 384])
        top8 = sb("top8", [P, 8])
        sel_b = sb("sel_b", [P, 384], BF16)
        nmax = sb("nmax", [P, 2, 16])
        den = sb("den", [P, 2, 16])
        rden = sb("rden", [P, 2, 16])
        cgt = sb("cgt", [P, NT, 24])
        cgt3 = cgt[:, :, :].rearrange("p t (h b) -> p t h b", b=3)
        hid = sb("hid", [P, 64])
        hid2 = sb("hid2", [P, 64])
        hid3 = sb("hid3", [P, 64])
        hid_v = sb("hid_v", [P, 8, CPAD])
        kc_t = sb("kc_t", [P, 2, 2, CPAD])
        comb = scr[:, 0:512].rearrange("p (h c) -> p h c", h=8)
        v_blk = scr[:, 512:1024].rearrange("p (h c) -> p h c", h=8)
        ps = ctx.enter_context(nc.psum_tensor("ps", [P, 8, 512], F32))

        gains = cur[:, 0:3 * KD]
        pos_c = cur[:, 3 * KD:3 * KD + 32].rearrange("p (v j) -> p v j", v=2)
        w2k = cur[:, 3 * KD + 32:3 * KD + 32 + 2 * HD]
        w2v = cur[:, 3 * KD + 32 + 2 * HD:]

        raw_in = [sem(f"raw_in{n}") for n in range(3)]
        hi_done = sem("hi_done")
        lo_done = sem("lo_done")
        slab_used = sem("slab_used")
        waited = sem("waited")
        x_loaded = sem("x_loaded")
        warmed = sem("warmed")
        rows_in = sem("rows_in")
        tables_in = sem("tables_in")
        setup_pe = sem("setup_pe")
        setup_v = sem("setup_v")
        setup_g = sem("setup_g")
        setup_w = sem("setup_w")
        cur_ready = sem("cur_ready")
        mix_ready = sem("mix_ready")
        x_new = sem("x_new")
        xt_ps = sem("xt_ps")
        hth = sem("hth")
        htl = sem("htl")
        ssq_done = sem("ssq_done")
        rstd_ready = sem("rstd_ready")
        sub_out = sem("sub_out")
        silu_done = sem("silu_done")
        act_done = sem("act_done")
        at_ps = sem("at_ps")
        ath = sem("ath")
        atl = sem("atl")
        proj_done = sem("proj_done")
        fill_ps = sem("fill_ps")
        fill_a = sem("fill_a")
        v_step = sem("v_step")
        cg_done = sem("cg_done")
        cmp_ps = sem("cmp_ps")
        gelu_t = sem("gelu_t")
        gate_t = sem("gate_t")
        gate_ready = sem("gate_ready")
        sc_ps = sem("sc_ps")
        exp_done = sem("exp_done")
        pt_ps = sem("pt_ps")
        pt_a = sem("pt_a")
        o_ps = sem("o_ps")
        ot_ps = sem("ot_ps")
        ot_h = sem("ot_h")
        y_ps = sem("y_ps")
        zsum = sem("zsum")
        out_done = sem("out_done")

        at_step = {}

        def of(s):
            return s if isinstance(s, tuple) else (0, s)

        def slot(s):
            return of(s)[1] % 3

        def wait_raw(eng, l, s):
            i, c = of(s)
            eng.wait_ge(raw_in[c % 3], l * (32 * LAYER_SLABS // 3) + i * 32 + 32 * (c // 3 + 1))

        def wait_used(eng, l, s):
            i, c = of(s)
            eng.wait_ge(slab_used, l * LAYER_SLABS + i * 3 + (c + 1 + 3))

        def splits(c):
            return c - (c > S_CK) - (c > S_CV)

        def wait_hi(eng, l, s):
            i, c = of(s)
            eng.wait_ge(hi_done, l * LAYER_SPLITS + i * 3 + splits(c) + 1)

        def wait_lo(eng, l, s):
            i, c = of(s)
            eng.wait_ge(lo_done, l * LAYER_SPLITS + i * 3 + splits(c) + 1 + 3)

        def apart(eng):
            eng.sem_inc(waited, 1)

        def wait_step(eng, l, name):
            eng.wait_ge(v_step, l * V_STEPS + at_step[name])

        def score_views(t):
            if t == 0:
                return ps[:, 4, :].rearrange("p (h c) -> p h c", h=4)
            return ps[:, 2:4, :].rearrange("p b (h c) -> p (b h) c", h=2)

        def prob_view(b, t):
            a, w = (0, P) if t == 0 else (512, SEQ)
            return prob[:, b, a:a + 4 * w].rearrange("p (h c) -> p h c", h=4)

        def heads_of(pair):
            if pair == "A":
                return QBLK["A"], KBLK["A"], 0, lambda h: A_V, A_Q
            if pair == "I":
                return QBLK["I"], KBLK["I"], 0, None, None
            if pair == "B":
                return QBLK["B"], KBLK["B"], 1, lambda h: B_V + h * HD, B_Q
            g = int(pair[1])
            v = C_VS if pair[0] == "S" else C_VW
            return QBLK["R"] + 2 * g, KBLK[pair[0]] + g, 0, lambda h: v + g * HD, C_Q + g * 4 * HD

        PT_FILLS = [(0, 0), (1, 0), (1, 1)]

        def fills_before(e):
            return 0 if e <= 1 else 1 + 3 * (e - 2)

        def pt_bank(e, f):
            return 6 if f == 1 else 4 if f == 2 and e == len(PAIRS) - 1 else 5

        PT_LAYER = fills_before(len(PAIRS))

        HID_T, K_OUT, V_OUT = slice(256, 320), slice(320, 352), slice(352, 416)

        def y_bank(g):
            return (g + 2) % 4

        def act_parts(i):
            if isinstance(i, int) and i == NSTEP - 1:
                return [h[:, KD - 2:KD, :].rearrange("p j c -> p (j c)") for h in (ht_hi, ht_lo)]
            return [h[:, :, :].rearrange("p j c -> p (j c)") for h in (at_hi, at_lo)]

        PT_ACT = 1 + 2 * (len(PAIRS) - 2)

        def acts_before(e):
            return 0 if e <= 1 else 1 + 2 * (e - 2)

        def copy_fill(copy, f):
            bank = 4 + f % 4
            if f >= len(FILLS):
                v = f - len(FILLS)
                src = ps[:, bank, :].rearrange("p (g c) -> p g c", g=2)
                copy(kvs[0:64, v, :, :], src[0:64], 1.0)
                copy(kvs[64:P, v, :, 0:SEQ - 1], src[64:P, :, 1:SEQ], 1.0)
                return
            (k0, b0), (k1, b1) = FILLS[f][1:]
            if k0 == "n":
                copy(qn_t[:, b0:b0 + 2, :].rearrange("p b c -> p (b c)"), ps[:, bank, :], ATT_SCALE)
                return
            if k0 == k1 != "k":
                copy(q_t[:, b0:b0 + 2, :].rearrange("p b c -> p (b c)"), ps[:, bank, :], ATT_SCALE if k0 == "qs" else 1.0)
                return
            for j, (kind, b) in enumerate(FILLS[f][1:]):
                src = ps[:, bank, j * SEQ:(j + 1) * SEQ]
                if kind == "k":
                    copy(k_t[0:64, b, 0, :], src[0:64], 1.0)
                    copy(k_t[64:P, b, 1, :], src[64:P], 1.0)
                else:
                    copy(q_t[:, b, :], src, ATT_SCALE if kind == "qs" else 1.0)

        def table_loads():
            for n, w in enumerate((cmp_w2_k, cmp_w2_k, cmp_w2_v)):
                yield w2_all[:, :, n, :], w.rearrange("l p d -> p l d")
            yield cos_s[:, :, :], cos_t.rearrange("(t p) c -> p t c", p=P)
            yield sin_s[:, :, :], sin_t.rearrange("(t p) c -> p t c", p=P)

        TABLE_DMAS = 5

        block = ctx.enter_context(nc.Block())

        @block.vector
        def _(dve):
            count = [0]

            def step(ins, name=None):
                count[0] += 1
                ins.then_inc(v_step, 1)
                if name is not None:
                    at_step[name] = count[0]

            def own(l):
                dve.wait_ge(v_step, l * V_STEPS + count[0])

            def convert(l, s, w=SLAB):
                wait_raw(dve, l, s)
                wait_hi(dve, l, s)
                i, c = of(s)
                wait_used(dve, l, (i, c - 3))
                n = slot(s)
                nc.vector.tensor_tensor(wlo[:, n, 0:w], raw[:, n, 0:w], whi[:, n, 0:w].bitcast(F32),
                                        ALU.subtract).then_inc(lo_done, 1)

            def prep(l, n, banks, blocks=range(4)):
                for k in [2 * b + j for b in blocks for j in range(2)]:
                    if k % 2 == 0:
                        dve.wait_ge(hth, (l * 3 + n) * KD + k + 2)
                    src = ps[:, banks[(k // 2) % 2], (k % 2) * SEQ:(k % 2 + 1) * SEQ]
                    nc.vector.scalar_tensor_tensor(ht_lo[:, k, :], src, gains[:, n * KD + k:n * KD + k + 1],
                                                   ht_hi[:, k, :].bitcast(F32), ALU.mult,
                                                   ALU.subtract).then_inc(htl, 1)

            def residual(l, n, bank0, factor, last_slab, banks=None):
                for g in range(4):
                    if g == 2 and banks:
                        convert(l, last_slab + 2)
                        prep(l, n + 1, banks, [0])
                    half, t = g // 2, g % 2
                    if g < 3:
                        dve.wait_ge(sub_out, (l * 3 + n) * 3 + g + 1)
                    else:
                        wait_used(dve, l, last_slab)
                    xv = x[:, t, half * 512:(half + 1) * 512]
                    nc.vector.scalar_tensor_tensor(xv, ps[:, bank0 + g, :], factor, xv, ALU.mult,
                                                   ALU.add).then_inc(x_new, 1)
                if banks:
                    prep(l, n + 1, banks, [1])

            def products(l, f, i):
                r = l * 2 + f
                for t in range(NT):
                    dve.wait_ge(silu_done, r * (2 * NSTEP) + i * 2 + t + 1)
                    if not (isinstance(i, int) and i == 0):
                        dve.wait_ge(at_ps, r * NSTEP + i)
                    bank = t + (6 if isinstance(i, int) and i == 0 else 0)
                    nc.vector.scalar_tensor_tensor(act[:, t, :], ps[:, bank, FSTEP:2 * FSTEP], rstd[:, t:t + 1],
                                                   sg[:, t, :], ALU.mult, ALU.mult).then_inc(act_done, 1)

            def act_rest(l, f, i):
                dve.wait_ge(ath, (l * 2 + f) * NSTEP + i + 1)
                hi, lo = act_parts(i)
                nc.vector.tensor_tensor(lo, ps[:, 2, :], hi.bitcast(F32), ALU.subtract).then_inc(atl, 1)

            def ffn(l, f):
                n, s0 = 2 * f, f * (FFN_SLABS + MIX_SLABS)
                if f == 0:
                    dve.wait_ge(cur_ready, l + 1)
                if f == 0:
                    prep(l, n, (2, 3), [0, 1])
                    convert(l, s0 + 1)
                prep(l, n, (2, 3) if f == 0 else (4, 5), [2, 3])
                convert(l, s0 + 2)
                dve.wait_ge(rstd_ready, (l * 3 + n) * 3 + 3)
                products(l, f, 0)
                convert(l, s0 + 3)
                act_rest(l, f, 0)
                def one(i):
                    r, c = (0, 3 * i) if isinstance(i, int) else (i, 0)
                    convert(l, (r, s0 + c + 1))
                    convert(l, (r, s0 + c + 2))
                    products(l, f, i)
                    if isinstance(i, int):
                        act_rest(l, f, i)
                    convert(l, (r, s0 + c + 3))
                    if not isinstance(i, int):
                        act_rest(l, f, i)

                with dve.Fori(1, NSTEP - 1) as i:
                    one(i)
                one(NSTEP - 1)
                residual(l, n, 4, 0.5, s0 + FFN_SLABS - 1, (2, 3) if f == 0 else None)

            def rope(l, u):
                if u == 0:
                    dve.wait_ge(tables_in, TABLE_DMAS * 16)
                dve.wait_ge(proj_done, l * 12 + 2 * u + 2)
                for c0, nh, b0, dup in ROPE[u]:
                    src = pr[:, :, c0:c0 + nh * HD].rearrange("p t (h c) -> p t h c", h=nh)
                    if dup:
                        dst = rs[:, :, b0:b0 + nh, 0:HD]
                    else:
                        dst = rs[:, :, b0:b0 + nh // 2, :].rearrange("p t b (e c) -> p t (b e) c", e=2)
                    tmp = rtmp[:, :, 0:nh, :]
                    cb = cos_s[:, :, :].unsqueeze(2).broadcast_to([P, NT, nh, HD])
                    sb_ = sin_s[:, :, :].unsqueeze(2).broadcast_to([P, NT, nh, HD])
                    own(l)
                    step(nc.vector.tensor_tensor(dst, src, cb, ALU.mult))
                    step(nc.vector.tensor_tensor(tmp[:, :, :, 0:32], src[:, :, :, 32:64], sb_[:, :, :, 0:32],
                                                 ALU.mult))
                    step(nc.vector.tensor_tensor(tmp[:, :, :, 32:64], src[:, :, :, 0:32], sb_[:, :, :, 32:64],
                                                 ALU.mult))
                    own(l)
                    step(nc.vector.tensor_tensor(dst, dst, tmp, ALU.add))
                    if dup:
                        own(l)
                        step(nc.vector.tensor_copy(rs[:, :, b0:b0 + nh, HD:2 * HD], dst))
                at_step["rope", u] = count[0]

            def fill_out(l, f):
                dve.wait_ge(fill_ps, l * NFILL + f + 1)
                copy_fill(lambda o, i, k: step(nc.vector.tensor_scalar(o, i, k, None, ALU.mult)), f)
                at_step["fill", f] = count[0]

            def cmp_windows(l):
                dve.wait_ge(fill_a, l * 7 + 7)
                dve.wait_ge(mix_ready, l * 2 + 2)
                own(l)
                for v in range(2):
                    for g in range(2):
                        for a in range(2):
                            win = kvs[:, v, g, 16 * a:16 * a + CMP_STRIDE * NCMP]\
                                .rearrange("p (n j r) -> p j n r", j=8, r=2)[:, :, :, 0]
                            o = cmpm[:, v, 8 * a:8 * a + 8, g * CPAD:g * CPAD + NCMP]
                            pb = pos_c[:, v, 8 * a:8 * a + 8].unsqueeze(2).broadcast_to([P, 8, NCMP])
                            step(nc.vector.tensor_tensor(o, win, pb, ALU.add), ("windows",))

            def hidden_rows(l):
                wait_used(dve, l, S_CV)
                step(nc.vector.tensor_copy(hid_rows, ps[0:2 * CPAD, 7, 0:2 * P]), ("hidden rows",))

            def hidden(l):
                dve.wait_ge(cmp_ps, l * 3 + 1)
                step(nc.vector.tensor_copy(hid[:, :], ps[:, 7, HID_T]))
                own(l)
                step(nc.vector.tensor_tensor(hid2[:, :], hid[:, :], hid[:, :], ALU.mult))
                own(l)
                step(nc.vector.tensor_scalar(hid2[:, :], hid2[:, :], 0.044715, 1.0, ALU.mult, ALU.add))
                own(l)
                step(nc.vector.tensor_tensor(hid2[:, :], hid2[:, :], hid[:, :], ALU.mult), ("gelu arg",))
                dve.wait_ge(gelu_t, l + 1)
                step(nc.vector.scalar_tensor_tensor(hid2[:, :], hid3[:, :], 1.0, hid[:, :], ALU.add, ALU.mult))
                own(l)
                step(nc.vector.tensor_scalar(hid[:, 0:32], hid2[:, 0:32], 0.5, None, ALU.mult))
                for g in range(2):
                    hv = hid2[:, 32 + g * CPAD:32 + (g + 1) * CPAD].unsqueeze(1).broadcast_to([P, 4, CPAD])
                    step(nc.vector.tensor_scalar(hid_v[:, 4 * g:4 * g + 4, :], hv, 0.5, None, ALU.mult),
                         ("hidden",))

            def compressed_out(l):
                dve.wait_ge(cmp_ps, l * 3 + 3)
                src = ps[:, 7, K_OUT].rearrange("p (g c) -> p g c", g=2)
                step(nc.vector.tensor_copy(kc_t[0:64, :, 0, :], src[0:64]))
                step(nc.vector.tensor_copy(kc_t[64:P, :, 1, :], src[64:P]), ("kc",))
                vb = ps[:, 7, V_OUT].unsqueeze(1).broadcast_to([P, 8, HD])
                step(nc.vector.tensor_tensor(v_blk[:, :, :], vb, hsel[:, :].unsqueeze(2).broadcast_to([P, 8, HD]),
                                             ALU.mult), ("v_blk",))

            def maxima(l, e):
                pair, b = PAIRS[e], e % 2
                own(l)
                for t in range(NT):
                    dve.wait_ge(sc_ps, l * 16 + 2 * e + t + 1)
                    if pair == "C":
                        continue
                    step(nc.vector.tensor_reduce(nmax[:, b, 4 * t:4 * t + 4], score_views(t), AX_X, ALU.max,
                                                 negate=True), ("max", e))
                if pair == "C":
                    sc = ps[:, 4, 0:256].rearrange("p (h c) -> p h c", h=16)
                    step(nc.vector.tensor_reduce(nmax[:, b, :], sc, AX_X, ALU.max, negate=True))
                    own(l)
                    o = prob[:, b, 0:256].rearrange("p (h c) -> p h c", h=16)
                    step(nc.vector.tensor_tensor(o, sc, nmax[:, b, :].unsqueeze(2).broadcast_to([P, 16, CPAD]),
                                                 ALU.add), ("max", e))

            def normed(l, e):
                pair, b = PAIRS[e], e % 2
                dve.wait_ge(o_ps, l * 7 + e)
                own(l)
                if pair == "C":
                    src = prob[:, b, 0:256].rearrange("p (h c) -> p h c", h=16)
                    step(nc.vector.tensor_reduce(den[:, b, :], src, AX_X, ALU.add))
                    own(l)
                    step(nc.vector.reciprocal(rden[:, b, :], den[:, b, :]))
                    own(l)
                    rt = rden[:, b, :].rearrange("p (t h) -> p t h", t=NT)
                    step(nc.vector.tensor_tensor(rt, rt, cgt3[:, :, :, 0], ALU.mult))
                    own(l)
                    for t in range(NT):
                        o = pr[:, t, C_Q:C_Q + 512].rearrange("p (h c) -> p h c", h=8)
                        i = ps[:, 7 - t, :].rearrange("p (h c) -> p h c", h=8)
                        step(nc.vector.tensor_tensor(o, i, rt[:, t, :].unsqueeze(2).broadcast_to([P, 8, HD]),
                                                     ALU.mult), ("norm", e))
                    return
                _, _, _, _, oc = heads_of(pair)
                rd = rden[:, b, 0:8]
                step(nc.vector.reciprocal(rd, den[:, b, 0:8]))
                own(l)
                o_in = ps[:, 7, :].rearrange("p (x c) -> p x c", c=HD)
                if pair in "AB":
                    o = pr[:, :, oc:oc + 256].rearrange("p t (h c) -> p t h c", h=4)
                    step(nc.vector.tensor_tensor(o, o_in.rearrange("p (t h) c -> p t h c", t=NT),
                                                 rd.rearrange("p (t h) -> p t h", t=NT).unsqueeze(3)
                                                 .broadcast_to([P, NT, 4, HD]), ALU.mult), ("norm", e))
                    return
                g, br = int(pair[1]), 1 if pair[0] == "S" else 2
                rt = rd.rearrange("p (t h) -> p t h", t=NT)
                step(nc.vector.tensor_tensor(rt, rt, cgt3[:, :, 4 * g:4 * g + 4, br], ALU.mult))
                own(l)
                step(nc.vector.tensor_tensor(comb[:, :, :], o_in, rd.unsqueeze(2).broadcast_to([P, 8, HD]),
                                             ALU.mult))
                own(l)
                o = pr[:, :, oc:oc + 256]
                step(nc.vector.tensor_tensor(o, o, comb[:, :, :].rearrange("p (t h) c -> p t (h c)", t=NT),
                                             ALU.add), ("norm", e))

            def index_scores(l):
                dve.wait_ge(exp_done, l * len(PAIRS) + 1)
                for t in range(NT):
                    wv = work[:, 0:P] if t == 0 else work[:, P:3 * P]
                    for h in range(4):
                        own(l)
                        step(nc.vector.scalar_tensor_tensor(
                            wv, prob_view(0, t)[:, h, :], pr[:, t, I_W + h:I_W + h + 1],
                            cmask[:, t, 0:(t + 1) * P] if h == 0 else wv, ALU.mult, ALU.add), ("index",))

            def select_round(l, n):
                t = n // 8
                wv = work[:, 0:P] if t == 0 else work[:, P:3 * P]
                own(l)
                apart(dve)
                step(nc.vector.max(top8[:, :], wv))
                own(l)
                apart(dve)
                step(nc.vector.match_replace(wv, top8[:, :], wv, TAKEN))
                if n == 15:
                    own(l)
                    step(nc.vector.tensor_scalar(sel_b[:, :], work[:, :], TAKEN, -BIG, ALU.not_equal, ALU.mult),
                         ("selected",))

            def branch_out(l, br, order, pieces=range(4)):
                for g in pieces:
                    half, t = g // 2, g % 2
                    if g < 3:
                        dve.wait_ge(y_ps, l * 9 + order * 3 + g + 1)
                    else:
                        wait_used(dve, l, FFN_SLABS + (M_BR, M_BR + 2, M_BR + 3)[order])
                    dve.wait_ge(gate_ready, l * 12 + 4 * br + 2 * half + t + 1)
                    gv = gate[:, t, br, half * 512:(half + 1) * 512]
                    bank = (y_bank(g), 4 + g, g)[order]
                    step(nc.vector.tensor_tensor(gv, ps[:, bank, :], gv, ALU.mult), ("gated", br, g))
                    if order == 2:
                        own(l)
                        dve.wait_ge(zsum, l * 4 + g + 1)
                        step(nc.vector.tensor_tensor(gv, gv, gate[:, t, 1, half * 512:(half + 1) * 512],
                                                     ALU.add), ("z", g))

            def turned_rest(l, n):
                k, bank = 2 * (n % 4), 4 + n % 4
                dve.wait_ge(ot_h, l * 8 + n + 1)
                step(nc.vector.tensor_tensor(ht_lo[:, k:k + 2, :].rearrange("p k c -> p (k c)"), ps[:, bank, :],
                                             ht_hi[:, k:k + 2, :].rearrange("p k c -> p (k c)").bitcast(F32),
                                             ALU.subtract), ("turned", n))

            def mixer(l):
                S = FFN_SLABS
                prep(l, 1, (2, 3), [2, 3])
                step(nc.vector.memset(cmpm[:, :, :, :], 0.0), ("cmpm zero",))
                for m in range(11):
                    convert(l, S + m + 2, LASTU * 8 if m + 2 == 10 else SLAB)
                    if m % 2:
                        rope(l, m // 2)
                rope(l, 5)
                dve.wait_ge(cg_done, l + 1)
                step(nc.vector.tensor_scalar(cgt[:, :, :], cgt[:, :, :], 0.5, 0.5, ALU.mult, ALU.add))
                own(l)
                step(nc.vector.tensor_tensor(cgt3[:, :, :, 0], cgt3[:, :, :, 0],
                                             valid[:, :].unsqueeze(2).broadcast_to([P, NT, 8]), ALU.mult))
                for f in range(1, NFILL, 2):
                    fill_out(l, f)
                cmp_windows(l)
                convert(l, S + 15)
                hidden_rows(l)
                hidden(l)
                convert(l, S + 16)
                compressed_out(l)
                convert(l, S + 17)
                rounds = [0, 1, 3, 2, 3, 3, 4, 0, 0, 0]
                done = 0
                for e in range(NPOS):
                    if 1 <= e - 2:
                        normed(l, e - 2)
                    if 2 <= e - 1 < len(PAIRS):
                        dve.wait_ge(pt_ps, l * PT_LAYER + fills_before(e - 1) + 2)
                        dve.wait_ge(o_ps, l * 7 + e - 2)
                        step(nc.vector.tensor_copy(p_t[:, 1, :], ps[:, 6, :]), ("pt", e - 1))
                    if 0 < e < len(PAIRS):
                        maxima(l, e)
                    if e == 1:
                        index_scores(l)
                    if e > 0:
                        convert(l, S + 17 + e)
                    for _ in range(rounds[e]):
                        select_round(l, done)
                        done += 1
                assert done == 16
                for n in range(4):
                    turned_rest(l, n)
                convert(l, S + 27)
                branch_out(l, 1, 0)
                convert(l, S + 28)
                branch_out(l, 2, 1, range(0, 2))
                convert(l, S + 29)
                branch_out(l, 2, 1, range(2, 4))
                branch_out(l, 0, 2, range(0, 3))
                turned_rest(l, 4)
                turned_rest(l, 5)
                branch_out(l, 0, 2, range(3, 4))
                convert(l, S + 30)
                for n in range(6, 8):
                    turned_rest(l, n)
                for m in range(31, 34):
                    convert(l, S + m)
                residual(l, 1, 0, 1.0, S + 32, (4, 5))

            dve.sem_inc(lo_done, 3)
            nc.vector.memset(k_t[:, :, :, :], 0.0).then_inc(setup_v, 1)
            dve.wait_ge(setup_pe, 1)
            nc.vector.tensor_copy(cols[:, :], ps[:, 0, 0:112]).then_inc(setup_v, 1)
            dve.wait_ge(setup_g, SETUP_G)
            convert(0, 0)
            with dve.Fori(0, DEPTH) as l:
                ffn(l, 0)
                mixer(l)
                ffn(l, 1)
            assert count[0] == V_STEPS, count[0]
            gf = gr[:, 0:D]
            dve.wait_ge(setup_w, 16)
            for t in range(NT):
                dve.wait_ge(rstd_ready, 3 * DEPTH * 3 + 3 + 2 * t)
                nc.vector.scalar_tensor_tensor(x[:, t, :], x[:, t, :], rstd[:, t:t + 1], gf, ALU.mult,
                                               ALU.mult).then_inc(x_new, 1)

        @block.gpsimd
        def _(pool):
            n = [0]

            def step(ins):
                n[0] += 1
                ins.then_inc(setup_g, 1)

            def own():
                pool.wait_ge(setup_g, n[0])

            step(nc.gpsimd.memset(mhalf[:, :], -0.5))
            assert n[0] == SETUP_WARM
            step(nc.gpsimd.memset(ident[:, :], 0.0))
            step(nc.gpsimd.memset(ident_b[:, :], 0.0))
            own()
            for m in (ident, ident_b):
                step(nc.gpsimd.affine_select(out=m[:, :], in_=m[:, :], compare_op=ALU.not_equal, fill=1.0, base=0,
                                             pattern=[[-1, P]], channel_multiplier=1))
            step(nc.gpsimd.memset(cmask[:, :, :], 0.0))
            step(nc.gpsimd.memset(cmask_b[:, :, :], 0.0))
            step(nc.gpsimd.memset(kmask_b[:, :, :], 0.0))
            step(nc.gpsimd.memset(valid[:, :], 1.0))
            step(nc.gpsimd.memset(hsel[:, :], 1.0))
            step(nc.gpsimd.memset(kc_t[:, :, :, :], 0.0))
            own()
            for m, fill in ((cmask, FILL), (cmask_b, -BIG)):
                step(nc.gpsimd.affine_select(out=m[:, :, :], in_=m[:, :, :], compare_op=ALU.is_ge, fill=fill, base=0,
                                             pattern=[[P, NT], [-1, SEQ]], channel_multiplier=1))
            step(nc.gpsimd.affine_select(out=kmask_b[:, :, :], in_=kmask_b[:, :, :], compare_op=ALU.is_ge, fill=-BIG,
                                         base=1 - CMP_BLOCK, pattern=[[P, NT], [-CMP_STRIDE, CPAD]],
                                         channel_multiplier=1))
            step(nc.gpsimd.affine_select(out=valid[:, :], in_=valid[:, :], compare_op=ALU.is_ge, fill=0.0,
                                         base=1 - CMP_BLOCK, pattern=[[P, NT]], channel_multiplier=1))
            step(nc.gpsimd.affine_select(out=hsel[:, :], in_=hsel[:, :], compare_op=ALU.is_ge, fill=0.0,
                                         base=0, pattern=[[-CPAD, 8]], channel_multiplier=1))
            own()
            step(nc.gpsimd.affine_select(out=hsel[:, :], in_=hsel[:, :], compare_op=ALU.is_ge, fill=0.0,
                                         base=CPAD - 1, pattern=[[CPAD, 8]], channel_multiplier=-1))
            assert n[0] == SETUP_G, n[0]
            pool.wait_ge(setup_v, 2)
            pool.wait_ge(x_loaded, 16)
            pool.sem_inc(x_new, 4)

            def layer_gains(l):
                nc.gpsimd.tensor_copy(gains.rearrange("p (n k) -> p n k", n=3),
                                      cols[:, 0:48].rearrange("p (n c) -> p n c", n=3)[:, :, ds(l * KD, KD)])\
                    .then_inc(cur_ready, 1)

            def mixer_constants(l):
                pool.wait_ge(tables_in, TABLE_DMAS * 16)
                nc.gpsimd.tensor_copy(pos_c, cols[:, 48:112].rearrange("p (v c) -> p v c", v=2)[:, :, ds(l * 16, 16)])\
                    .then_inc(mix_ready, 1)
                nc.gpsimd.tensor_copy(cur[:, 3 * KD + 32:].unsqueeze(1),
                                      w2_all[:, ds(l, 1), :, :].rearrange("p a b c -> p a (b c)"))\
                    .then_inc(mix_ready, 1)

            def norm(p):
                pool.wait_ge(ssq_done, p * NT + NT)
                apart(pool)
                nc.gpsimd.tensor_scalar(msq[:, :], ssq[:, :], 1.0 / D, EPS, ALU.mult, ALU.add).then_inc(rstd_ready, 1)
                pool.wait_ge(rstd_ready, p * 3 + 1)
                nc.gpsimd.tensor_tensor(rstd[:, :], msq[:, :], mhalf[:, :], ALU.pow).then_inc(rstd_ready, 1)
                pool.wait_ge(rstd_ready, p * 3 + 2)
                apart(pool)
                nc.gpsimd.tensor_scalar(hrstd[:, :], rstd[:, :], 0.5, None, ALU.mult).then_inc(rstd_ready, 1)

            with pool.Fori(0, DEPTH) as l:
                pool.wait_ge(x_new, l * 12 + 1)
                layer_gains(l)
                norm(l * 3)
                mixer_constants(l)
                norm(l * 3 + 1)
                for w in range(6):
                    for t in range(NT):
                        pool.wait_ge(gate_t, l * 12 + 2 * w + t + 1)
                        apart(pool)
                        gv = gate[:, t, w // 2, (w % 2) * 512:(w % 2 + 1) * 512]
                        nc.gpsimd.tensor_scalar(gv, gv, 0.5, 0.5, ALU.mult, ALU.add).then_inc(gate_ready, 1)
                for g in range(4):
                    half, t = g // 2, g % 2
                    wait_step(pool, l, ("gated", 2, g))
                    a, b = (gate[:, t, br, half * 512:(half + 1) * 512] for br in (1, 2))
                    nc.gpsimd.tensor_tensor(a, a, b, ALU.add).then_inc(zsum, 1)
                norm(l * 3 + 2)
            p = 3 * DEPTH
            pool.wait_ge(ssq_done, p * NT + 2)
            apart(pool)
            nc.gpsimd.tensor_scalar(msq[:, :], last_ms[:, 0:2], EPS, None, ALU.add).then_inc(rstd_ready, 1)
            for t in range(NT):
                pool.wait_ge(ssq_done, p * NT + 3 + t)
                pool.wait_ge(rstd_ready, p * 3 + 1 + 2 * t)
                c = slice(t, t + 1)
                nc.gpsimd.tensor_tensor(msq[:, c], msq[:, c], last_ms[:, 2 + t:3 + t], ALU.add)\
                    .then_inc(rstd_ready, 1)
                pool.wait_ge(rstd_ready, p * 3 + 2 + 2 * t)
                nc.gpsimd.tensor_tensor(rstd[:, c], msq[:, c], mhalf[:, c], ALU.pow).then_inc(rstd_ready, 1)

        @block.scalar
        def _(eng):
            tables = list(table_loads())
            eng.dma_start(rows[:, :], rows_dram).then_inc(rows_in, 16)
            for dst, src in tables[0:1]:
                eng.dma_start(dst, src).then_inc(tables_in, 16)
            eng.dma_start(x[:, :, :], x_in.rearrange("a (t p) d -> p (a t) d", p=P)).then_inc(x_loaded, 16)

            def convert(l, s, w=SLAB):
                wait_raw(eng, l, s)
                i, c = of(s)
                wait_used(eng, l, (i, c - 3))
                n = slot(s)
                nc.scalar.activation(whi[:, n, 0:w], raw[:, n, 0:w], ACT.Copy).then_inc(hi_done, 1)

            def squares(p):
                for t in range(NT):
                    nc.scalar.activation(p_t[:, t, :].bitcast(BF16), x[:, t, :], ACT.Square,
                                         accum_out=ssq[:, t:t + 1]).then_inc(ssq_done, 1)

            def prep(l, n, banks, blocks=range(4)):
                for k in [2 * b + j for b in blocks for j in range(2)]:
                    eng.wait_ge(xt_ps, (l * 3 + n) * 4 + k // 2 + 1)
                    src = ps[:, banks[(k // 2) % 2], (k % 2) * SEQ:(k % 2 + 1) * SEQ]
                    nc.scalar.activation(ht_hi[:, k, :], src, ACT.Copy,
                                         scale=gains[:, n * KD + k:n * KD + k + 1]).then_inc(hth, 1)
                if 3 in blocks:
                    squares(l * 3 + n)

            def silu(l, f, i, first):
                r, s0 = l * 2 + f, f * (FFN_SLABS + MIX_SLABS)
                wait_used(eng, l, s0 + 1 if first else s0 + 3 * i if isinstance(i, int) else (i, s0))
                for t in range(NT):
                    if not first:
                        eng.wait_ge(act_done, r * (2 * NSTEP) + i * 2 + t - 1)
                    nc.scalar.activation(sg[:, t, :], ps[:, t + (6 if first else 0), 0:FSTEP], ACT.Silu,
                                         scale=rstd[:, t:t + 1]).then_inc(silu_done, 1)

            def act_round(l, f, i):
                eng.wait_ge(at_ps, (l * 2 + f) * NSTEP + i + 1)
                nc.scalar.activation(act_parts(i)[0], ps[:, 2, :], ACT.Copy).then_inc(ath, 1)

            def ffn(l, f):
                n, s0 = 2 * f, f * (FFN_SLABS + MIX_SLABS)
                if f == 0:
                    eng.wait_ge(warmed, l + 1)
                    warm_up()
                    eng.wait_ge(cur_ready, l + 1)
                if f == 0:
                    prep(l, n, (2, 3), [0, 1])
                    convert(l, s0 + 1)
                    prep(l, n, (2, 3), [2, 3])
                else:
                    prep(l, n, (4, 5))
                convert(l, s0 + 2)
                eng.wait_ge(rstd_ready, (l * 3 + n) * 3 + 3)
                silu(l, f, 0, True)
                convert(l, s0 + 3)
                act_round(l, f, 0)
                def one(i):
                    r, c = (0, 3 * i) if isinstance(i, int) else (i, 0)
                    convert(l, (r, s0 + c + 1))
                    convert(l, (r, s0 + c + 2))
                    silu(l, f, i, False)
                    convert(l, (r, s0 + c + 3))
                    act_round(l, f, i)

                with eng.Fori(1, NSTEP - 1) as i:
                    one(i)
                one(NSTEP - 1)
                if f == 0:
                    convert(l, s0 + FFN_SLABS + 1)

            def project_out(l, u):
                w = 512 if u < 5 else LASTU
                wait_used(eng, l, FFN_SLABS + (2 * u + 1 if u < 5 else 10))
                for t in range(NT):
                    nc.scalar.activation(pr[:, t, u * 512:u * 512 + w], ps[:, 2 * (u % 2) + t, 0:w], ACT.Copy,
                                         scale=rstd[:, t:t + 1]).then_inc(proj_done, 1)

            def gates(l, w):
                wait_used(eng, l, FFN_SLABS + (12 if w == 0 else 16 + 2 * (w - 1)))
                for t in range(NT):
                    nc.scalar.activation(gate[:, t, w // 2, (w % 2) * 512:(w % 2 + 1) * 512], ps[:, t, :], ACT.Tanh,
                                         scale=hrstd[:, t:t + 1]).then_inc(gate_t, 1)

            def exps(l, e):
                pair, b = PAIRS[e], e % 2
                if pair == "I":
                    for t in range(NT):
                        eng.wait_ge(sc_ps, l * 16 + 2 * e + t + 1)
                        ins = nc.scalar.activation(prob_view(b, t), score_views(t), ACT.Relu, scale=IDX_SCALE)
                    ins.then_inc(exp_done, 1)
                    return
                wait_step(eng, l, ("max", e))
                if pair == "C":
                    pv = prob[:, b, 0:256]
                    nc.scalar.activation(pv, pv, ACT.Exp).then_inc(exp_done, 1)
                    return
                if e == 2:
                    wait_step(eng, l, ("index",))
                for t in range(NT):
                    for h in range(4):
                        ins = nc.scalar.activation(prob_view(b, t)[:, h, :], score_views(t)[:, h, :], ACT.Exp,
                                                   bias=nmax[:, b, 4 * t + h:4 * t + h + 1],
                                                   accum_out=den[:, b, 4 * t + h:4 * t + h + 1])
                ins.then_inc(exp_done, 1)

            def prob_out(l, e, f):
                eng.wait_ge(pt_ps, l * PT_LAYER + fills_before(e) + f + 1)
                if e > 1:
                    eng.wait_ge(o_ps, l * 7 + e - 1)
                w = 256 if PAIRS[e] == "C" else 512
                nc.scalar.activation(p_t[:, f, 0:w], ps[:, pt_bank(e, f), 0:w], ACT.Copy).then_inc(pt_a, 1)

            def turned(l, n):
                k, bank = 2 * (n % 4), 4 + n % 4
                eng.wait_ge(ot_ps, l * 8 + n + 1)
                nc.scalar.activation(ht_hi[:, k:k + 2, :].rearrange("p k c -> p (k c)"), ps[:, bank, :],
                                     ACT.Copy).then_inc(ot_h, 1)

            def mixer(l):
                S = FFN_SLABS
                prep(l, 1, (2, 3))
                for m in range(11):
                    convert(l, S + m + 2, LASTU * 8 if m + 2 == 10 else SLAB)
                    if m == 1:
                        eng.wait_ge(rstd_ready, (l * 3 + 1) * 3 + 3)
                    if m % 2:
                        project_out(l, m // 2)
                project_out(l, 5)
                eng.wait_ge(proj_done, l * 12 + 12)
                nc.scalar.activation(cgt[:, :, :], pr[:, :, C_G:C_G + 24], ACT.Tanh, scale=0.5).then_inc(cg_done, 1)
                for f in range(0, NFILL, 2):
                    eng.wait_ge(fill_ps, l * NFILL + f + 1)
                    copy_fill(lambda o, i, k: copied.append(nc.scalar.activation(o, i, ACT.Copy, scale=k)), f)
                    copied.pop().then_inc(fill_a, 1)
                    copied.clear()
                gates(l, 0)
                convert(l, S + 15)
                convert(l, S + 16)
                wait_step(eng, l, ("gelu arg",))
                nc.scalar.activation(hid3[:, :], hid2[:, :], ACT.Tanh, scale=0.7978845608028654).then_inc(gelu_t, 1)
                convert(l, S + 17)
                for e in range(NPOS):
                    if e in (2, 4, 6, 8):
                        gates(l, e // 2)
                    if 1 <= e - 1 < len(PAIRS):
                        prob_out(l, e - 1, 0)
                    if e > 0:
                        convert(l, S + 17 + e)
                    if 2 <= e - 1 < len(PAIRS):
                        prob_out(l, e - 1, 2)
                    if e < len(PAIRS):
                        exps(l, e)
                turned(l, 0)
                turned(l, 1)
                gates(l, 5)
                turned(l, 2)
                turned(l, 3)
                for m in range(27, 30):
                    convert(l, S + m)
                for n in range(4, 6):
                    turned(l, n)
                convert(l, S + 30)
                for n in range(6, 8):
                    turned(l, n)
                for m in range(31, 35):
                    convert(l, S + m)

            def warm_up():
                nc.scalar.activation(warm[:, :], mhalf[:, 0:1], ACT.Copy).then_inc(warmed, 1)

            copied = []
            eng.wait_ge(setup_g, SETUP_WARM)
            warm_up()
            convert(0, 0)
            for dst, src in tables[1:]:
                eng.dma_start(dst, src).then_inc(tables_in, 16)
            with eng.Fori(0, DEPTH) as l:
                ffn(l, 0)
                mixer(l)
                ffn(l, 1)
            for g in range(4):
                half, t = g // 2, g % 2
                eng.wait_ge(x_new, 3 * DEPTH * 4 + g + 1)
                nc.scalar.activation(p_t[:, t, half * 256:(half + 1) * 256].bitcast(BF16),
                                     x[:, t, half * 512:(half + 1) * 512], ACT.Square, scale=D ** -0.5,
                                     accum_out=last_ms[:, g:g + 1]).then_inc(ssq_done, 1)

        @block.tensor
        def _(pe):
            def three(o, xh, xl, wh, wl, start, stop):
                nc.tensor.matmul(o, xh, wh, start=start, stop=False)
                nc.tensor.matmul(o, xh, wl, start=False, stop=False)
                return nc.tensor.matmul(o, xl, wh, start=False, stop=stop)

            def ready(l, s):
                wait_hi(pe, l, s)
                wait_lo(pe, l, s)

            def prep(l, n, banks, blocks=range(4)):
                for b in blocks:
                    pe.wait_ge(x_new, (l * 3 + n) * 4 + 2 * (b // 2) + 2)
                    if b >= 2:
                        pe.wait_ge(htl, (l * 3 + n) * KD + 2 * (b - 1))
                    for j in range(2):
                        for t in range(NT):
                            ins = nc.tensor.transpose(ps[:, banks[b % 2], j * SEQ + t * P:j * SEQ + (t + 1) * P],
                                                      x[:, t, (2 * b + j) * P:(2 * b + j + 1) * P], ident[:, :])
                    ins.then_inc(xt_ps, 1)

            def wide(l, s, k0, nk, banks, width, kstart, kstop, first=False, n=0, halfway=None):
                ready(l, s)
                wv = whi[:, slot(s), 0:nk * width].rearrange("p (k c) -> p k c", k=nk)
                wr = wlo[:, slot(s), 0:nk * width].rearrange("p (k c) -> p k c", k=nk)
                for kk in range(nk):
                    k = k0 + kk
                    if halfway and kk == nk // 2:
                        halfway()
                    if first:
                        pe.wait_ge(htl, (l * 3 + n) * KD + k + 1)
                    for t in range(NT):
                        ins = three(ps[:, banks[t], 0:width], ht_hi[:, k, t * P:(t + 1) * P],
                                    ht_lo[:, k, t * P:(t + 1) * P], wv[:, kk, :], wr[:, kk, :],
                                    k == kstart, k == kstop)
                ins.then_inc(slab_used, 1)

            def tall(l, s, hi, lo, k0, bank0, start, stop, signal=None, between={}, bank_of=lambda g: g):
                ready(l, s)
                wv = whi[:, slot(s), :].rearrange("p (j c) -> p j c", j=2)
                wr = wlo[:, slot(s), :].rearrange("p (j c) -> p j c", j=2)
                for g in range(4):
                    half, t = g // 2, g % 2
                    if g in between:
                        between[g]()
                    for j in range(2):
                        ins = three(ps[:, bank0 + bank_of(g), :], hi[:, k0 + j, t * P:(t + 1) * P],
                                    lo[:, k0 + j, t * P:(t + 1) * P], wv[:, j, half * 512:(half + 1) * 512],
                                    wr[:, j, half * 512:(half + 1) * 512], start and j == 0, stop and j == 1)
                    if g == 3:
                        ins.then_inc(slab_used, 1)
                    elif signal is not None:
                        ins.then_inc(signal, 1)

            def gate_up(l, f, i, first=False, halfway=None):
                r, s0 = l * 2 + f, f * (FFN_SLABS + MIX_SLABS)
                if not first:
                    pe.wait_ge(act_done, r * (2 * NSTEP) + i * 2)
                for a in range(2):
                    s = s0 + a if first else s0 + 3 * i - 1 + a if isinstance(i, int) else (i, s0 - 1 + a)
                    wide(l, s, 4 * a, 4, (6, 7) if first else (0, 1), 512, 0, KD - 1, first, 2 * f,
                         halfway if a == 0 else None)

            def turn(l, f, i):
                r = l * 2 + f
                pe.wait_ge(act_done, r * (2 * NSTEP) + i * 2 + 2)
                for j in range(2):
                    for t in range(NT):
                        ins = nc.tensor.transpose(ps[:, 2, j * SEQ + t * P:j * SEQ + (t + 1) * P],
                                                  act[:, t, j * P:(j + 1) * P], ident[:, :])
                ins.then_inc(at_ps, 1)

            def down(l, f, i, s, start=False, between={}):
                pe.wait_ge(atl, (l * 2 + f) * NSTEP + i + 1)
                if isinstance(i, int) and i == NSTEP - 1:
                    tall(l, s, ht_hi, ht_lo, KD - 2, 4, False, True, sub_out, between)
                else:
                    tall(l, s, at_hi, at_lo, 0, 4, start, False, None, between)

            def ffn(l, f):
                s0, last = f * (FFN_SLABS + MIX_SLABS), NSTEP - 1
                banks = (2, 3) if f == 0 else (4, 5)
                if f == 0:
                    prep(l, 0, banks, [0, 1])
                gate_up(l, f, 0, True, lambda: prep(l, 2 * f, banks, [2, 3]))
                wide(l, s0 + 2, 0, 4, (0, 1), 512, 0, KD - 1)
                turn(l, f, 0)
                wide(l, s0 + 3, 4, 4, (0, 1), 512, 0, KD - 1)
                down(l, f, 0, s0 + 4, start=True)
                turn(l, f, 1)
                with pe.Fori(2, last) as i:
                    gate_up(l, f, i)
                    down(l, f, i - 1, (i, s0 + 1))
                    turn(l, f, i)
                gate_up(l, f, last)
                down(l, f, last - 1, s0 + 3 * last + 1, between={2: lambda: turn(l, f, last)})
                if f == 0:
                    down(l, f, last, s0 + FFN_SLABS - 1, between={3: lambda: prep(l, 1, (2, 3), [0])})
                    prep(l, 1, (2, 3), [1])
                else:
                    down(l, f, last, s0 + FFN_SLABS - 1)

            def fill(l, f):
                bank = 4 + f % 4
                if f >= 4:
                    if f % 2:
                        wait_step(pe, l, ("fill", f - 4))
                    else:
                        pe.wait_ge(fill_a, l * 7 + (f - 4) // 2 + 1)
                for j in range(2):
                    for t in range(NT):
                        cols_out = slice(j * SEQ + t * P, j * SEQ + (t + 1) * P)
                        if f < len(FILLS):
                            b = FILLS[f][0][j]
                            src = rs[:, t, b, :] if b < NRB else \
                                pr[:, t, C_Q + (b - NRB) * P:C_Q + (b - NRB + 1) * P]
                            ins = nc.tensor.transpose(ps[:, bank, cols_out], src, ident[:, :])
                        else:
                            c0 = (C_KC if f == len(FILLS) else C_VC) + j * HD
                            for p0 in (0, HD):
                                ins = nc.tensor.matmul(ps[p0:p0 + HD, bank, cols_out], pr[:, t, c0:c0 + HD],
                                                       ident[:, :], start=True, stop=True)
                ins.then_inc(fill_ps, 1)

            def compress(l, v):
                s = FFN_SLABS + M_CK + v
                wait_raw(pe, l, s)
                w1 = raw[:, slot(s), :].rearrange("p (j c) -> p j c", j=16)
                for j in range(16):
                    ins = nc.tensor.matmul(ps[0:2 * CPAD, 7, v * P:(v + 1) * P], cmpm[:, v, j, :], w1[:, j, :],
                                           start=j == 0, stop=j == 15)
                ins.then_inc(slab_used, 1)

            def scores(l, e):
                pair = PAIRS[e]
                if e:
                    pe.wait_ge(exp_done, l * len(PAIRS) + e)
                qb, kb, kstep, _, _ = heads_of(pair) if pair != "C" else (0,) * 5
                if pair == "A":
                    wait_step(pe, l, ("selected",))
                for t in range(NT):
                    if pair == "C":
                        nc.tensor.matmul(ps[:, 4, t * P:(t + 1) * P], ident_b[:, :],
                                         kmask_b[:, t, :].unsqueeze(1).broadcast_to([P, 8, CPAD]),
                                         start=t == 0, stop=False, skip_group_check=True)
                        for j in range(4):
                            ins = nc.tensor.matmul(ps[:, 4, t * P + 32 * j:t * P + 32 * j + 32],
                                                   qn_t[:, j, t * P:(t + 1) * P],
                                                   kc_t[:, j // 2, :, :].rearrange("p a c -> p (a c)"),
                                                   start=False, stop=t == 1 and j == 3, skip_group_check=True)
                        ins.then_inc(sc_ps, 1)
                        continue
                    nk = (t + 1) * P
                    for b in range(t + 1):
                        bank = 4 if t == 0 else 2 + b
                        nh = 512 // nk
                        for j in range(nh // 2):
                            jj = b + j if t == 1 else j
                            ins = nc.tensor.matmul(ps[:, bank, j * 2 * nk:(j + 1) * 2 * nk],
                                                   q_t[:, qb + jj, t * P:(t + 1) * P],
                                                   k_t[:, kb + kstep * jj, :, 0:nk], start=j == 0,
                                                   stop=pair == "I" and j == nh // 2 - 1, skip_group_check=True)
                        if pair == "A":
                            mk = sel_b[:, 0:P] if t == 0 else sel_b[:, P:3 * P]
                            nc.tensor.matmul(ps[:, bank, :], ident_b[:, :], mk.unsqueeze(1).broadcast_to([P, nh, nk]),
                                             start=False, stop=False, skip_group_check=True)
                        if pair != "I":
                            o = ps[:, bank, :].rearrange("p (h c) -> p h c", h=nh)[:, :, nk - P:nk]
                            mk = cmask_b[:, t, nk - P:nk].unsqueeze(1).broadcast_to([P, nh, P])
                            ins = nc.tensor.matmul(o, ident_b[:, :], mk, start=False, stop=True,
                                                   skip_group_check=True)
                    ins.then_inc(sc_ps, 1)

            def turn_probs(l, e, f):
                pair, b = PAIRS[e], e % 2
                if f == 0:
                    pe.wait_ge(exp_done, l * len(PAIRS) + e + 1)
                if pair == "C":
                    for t in range(NT):
                        ins = nc.tensor.transpose(ps[:, 5, t * P:(t + 1) * P], prob[:, b, t * P:(t + 1) * P],
                                                  ident[:, :])
                    ins.then_inc(pt_ps, 1)
                    return
                if f == 1 and PAIRS[e - 1] == "C":
                    wait_step(pe, l, ("norm", e - 1))
                if f == 2 and pt_bank(e, 2) == pt_bank(e, 0):
                    pe.wait_ge(pt_a, l * PT_ACT + acts_before(e) + 1)
                t, kt = PT_FILLS[f]
                for h in range(4):
                    ins = nc.tensor.transpose(ps[:, pt_bank(e, f), h * P:(h + 1) * P],
                                              prob_view(b, t)[:, h, kt * P:(kt + 1) * P], ident[:, :])
                ins.then_inc(pt_ps, 1)

            def weighted(l, e):
                pair = PAIRS[e]
                pe.wait_ge(pt_a, l * PT_ACT + acts_before(e + 1))
                if e > 1:
                    wait_step(pe, l, ("pt", e))
                    wait_step(pe, l, ("norm", e - 1))
                if pair == "C":
                    for t in range(NT):
                        ins = nc.tensor.matmul(ps[:, 7 - t, :], p_t[:, 0, t * P:(t + 1) * P],
                                               v_blk[:, :, :].rearrange("p h c -> p (h c)"), start=True, stop=True)
                    ins.then_inc(o_ps, 1)
                    return
                vcol = heads_of(pair)[3]
                for t in range(NT):
                    for h in range(4):
                        for f, (ft, kt) in enumerate(PT_FILLS):
                            if ft != t:
                                continue
                            ins = nc.tensor.matmul(ps[:, 7, (t * 4 + h) * HD:(t * 4 + h + 1) * HD],
                                                   p_t[:, f, h * P:(h + 1) * P],
                                                   pr[:, kt, vcol(h):vcol(h) + HD], start=kt == 0, stop=kt == t,
                                                   skip_group_check=True)
                ins.then_inc(o_ps, 1)

            def turn_out(l, n):
                for j in range(2):
                    for t in range(NT):
                        k = 2 * (n % 4) + j
                        if n < 4:
                            c0 = (B_Q + k * P) if k < 2 else (C_Q + (k - 2) * P) if k < 6 else (A_Q + (k - 6) * P)
                            src = pr[:, t, c0:c0 + P]
                        else:
                            src = gate[:, t, 0, k * P:(k + 1) * P]
                        ins = nc.tensor.transpose(ps[:, 4 + n % 4, j * SEQ + t * P:j * SEQ + (t + 1) * P], src,
                                                  ident[:, :])
                ins.then_inc(ot_ps, 1)

            def mixer(l):
                S = FFN_SLABS
                for u in range(5):
                    banks = (2 * (u % 2), 2 * (u % 2) + 1)
                    if u >= 2:
                        pe.wait_ge(proj_done, l * 12 + 2 * (u - 1))
                    for a in range(2):
                        wide(l, S + 2 * u + a, 4 * a, 4, banks, 512, 0, KD - 1, u == 0, 1,
                             (lambda: prep(l, 1, (2, 3), [2, 3])) if u == a == 0 else None)
                pe.wait_ge(proj_done, l * 12 + 8)
                wide(l, S + 10, 0, KD, (2, 3), LASTU, 0, KD - 1)
                wait_step(pe, l, ("rope", 3))
                for f in range(T1):
                    if f == 0:
                        pe.wait_ge(proj_done, l * 12 + 10)
                    fill(l, f)
                wide(l, S + 11, 0, 4, (0, 1), 512, 0, KD - 1)
                pe.wait_ge(proj_done, l * 12 + 12)
                wait_step(pe, l, ("rope", 5))
                for f in range(T1, NFILL):
                    fill(l, f)
                wide(l, S + 12, 4, 4, (0, 1), 512, 0, KD - 1)
                wait_step(pe, l, ("windows",))
                compress(l, 0)
                compress(l, 1)

                def turn_hidden():
                    wait_step(pe, l, ("hidden rows",))
                    apart(pe)
                    for v in range(2):
                        ins = nc.tensor.transpose(ps[:, 7, HID_T][:, 2 * CPAD * v:2 * CPAD * (v + 1)],
                                                  hid_rows[:, v * P:(v + 1) * P], ident[0:2 * CPAD, 0:2 * CPAD])
                    ins.then_inc(cmp_ps, 1)

                def compressed():
                    wait_step(pe, l, ("hidden",))
                    nc.tensor.matmul(ps[:, 7, K_OUT], w2k, hid[:, 0:32], start=True, stop=True).then_inc(cmp_ps, 1)
                    nc.tensor.matmul(ps[:, 7, V_OUT], hid_v[:, :, :].rearrange("p h c -> p (h c)"), w2v, start=True,
                                     stop=True).then_inc(cmp_ps, 1)

                def outputs_turned():
                    wait_step(pe, l, ("norm", len(PAIRS) - 1))
                    turn_out(l, 0)
                    turn_out(l, 1)

                wait_step(pe, l, ("fill", 9))
                pe.wait_ge(fill_a, l * 7 + 7)
                for e in range(NPOS):
                    if e == 1:
                        wait_step(pe, l, ("v_blk",))
                    if 1 <= e - 1 < len(PAIRS):
                        turn_probs(l, e - 1, 0)
                        if e - 1 > 2:
                            turn_probs(l, e - 1, 1)
                    if e < len(PAIRS):
                        scores(l, e)
                    if e - 1 == 2:
                        turn_probs(l, e - 1, 1)
                    if 2 <= e - 1 < len(PAIRS):
                        turn_probs(l, e - 1, 2)
                    if e % 2 == 0:
                        pe.wait_ge(gate_t, l * 12 + e + 2)
                    if e == 0:
                        turn_hidden()
                    wide(l, S + 15 + e, 4 * (e % 2), 4, (0, 1), 512, 0, KD - 1,
                         halfway={0: compressed, NPOS - 1: outputs_turned}.get(e))
                    if 1 <= e - 1 < len(PAIRS):
                        weighted(l, e - 1)
                turn_out(l, 2)
                turn_out(l, 3)
                wait_step(pe, l, ("turned", 0))
                tall(l, S + 25, ht_hi, ht_lo, 0, 0, True, True, y_ps,
                     {2: lambda: pe.wait_ge(gate_t, l * 12 + 12)}, bank_of=y_bank)
                wait_step(pe, l, ("turned", 3))
                tall(l, S + 26, ht_hi, ht_lo, 2, 4, True, False)
                tall(l, S + 27, ht_hi, ht_lo, 4, 4, False, True, y_ps)
                wait_step(pe, l, ("gated", 1, 3))

                def turn_z(*banks):
                    for n in banks:
                        wait_step(pe, l, ("z", 1 if n < 6 else 3))
                        turn_out(l, n)

                tall(l, S + 28, ht_hi, ht_lo, 6, 0, True, True, y_ps, {3: lambda: turn_z(4, 5)})
                for a in range(4):
                    if a == 1:
                        turn_z(6, 7)
                    wait_step(pe, l, ("turned", 4 + a))
                    if a == 0:
                        tall(l, S + 29, ht_hi, ht_lo, 0, 0, True, False, None,
                             {3: lambda: wait_step(pe, l, ("gated", 0, 3))})
                    elif a < 3:
                        tall(l, S + 29 + a, ht_hi, ht_lo, 2 * a, 0, False, False)
                    else:
                        tall(l, S + 32, ht_hi, ht_lo, 6, 0, False, True, sub_out,
                             {3: lambda: prep(l, 2, (4, 5), [0])})
                prep(l, 2, (4, 5), [1])

            pe.sem_inc(slab_used, 3)
            pe.wait_ge(rows_in, 16)
            pe.wait_ge(setup_g, 5)
            nc.tensor.transpose(ps[:, 0, 0:112], rows[:, :], ident[0:112, 0:112]).then_inc(setup_pe, 1)
            with pe.Fori(0, DEPTH) as l:
                ffn(l, 0)
                mixer(l)
                ffn(l, 1)

        @block.sync
        def _(sp):
            def load(l, s, parts):
                i, c = of(s)
                before = c - 3
                if before in (S_CK, S_CV):
                    wait_used(sp, l, before)
                else:
                    b = splits(before) if before >= 0 else before
                    sp.wait_ge(lo_done, l * LAYER_SPLITS + i * 3 + b + 1 + 3)
                for dst, src in parts:
                    sp.dma_start(dst, src).then_inc(raw_in[slot(s)], 16)

            def rows_cols(w, l, r0, nk, c0, n):
                v = w[ds(l, 1), ds(r0, nk * P), ds(c0, n)]
                return v.rearrange("a (k p) c -> p (a k) c", p=P)

            def slab(s, nk):
                return lambda w: raw[:, slot(s), 0:nk * w].rearrange("p (k c) -> p k c", k=nk)

            def load_gate_up(l, s, wg, wu, a, col):
                v = slab(s, 4)(512)
                load(l, s, [(v[:, :, 0:FSTEP], rows_cols(wg, l, 512 * a, 4, col, FSTEP)),
                            (v[:, :, FSTEP:], rows_cols(wu, l, 512 * a, 4, col, FSTEP))])

            def load_halves(l, s, w, r0, nk, c0, n):
                v = slab(s, nk)(n)
                h = nk // 2
                load(l, s, [(v[:, 0:h, :], rows_cols(w, l, r0, h, c0, n)),
                            (v[:, h:nk, :], rows_cols(w, l, r0 + h * P, h, c0, n))])

            def ffn(l, f, wg, wu, wd):
                s0 = f * (FFN_SLABS + MIX_SLABS)
                for a in range(2):
                    load_gate_up(l, s0 + a, wg, wu, a, 0)
                with sp.Fori(1, NSTEP) as i:
                    for a in range(2):
                        load_gate_up(l, (i, s0 - 1 + a), wg, wu, a, i * FSTEP)
                    load_halves(l, (i, s0 + 1), wd, i * FSTEP - FSTEP, 2, 0, D)
                load_halves(l, s0 + FFN_SLABS - 1, wd, DFF - FSTEP, 2, 0, D)

            def mixer(l):
                S = FFN_SLABS
                for m in range(10):
                    load_halves(l, S + m, w_in, 512 * (m % 2), 4, 512 * (m // 2), 512)
                load_halves(l, S + 10, w_in, 0, 8, 5 * 512, LASTU)
                for m in (11, 12):
                    load_halves(l, S + m, w_in, 512 * (m - 11), 4, M_G, 512)
                load_halves(l, S + M_CK, cmp_w1_k, 0, 16, 0, P)
                load_halves(l, S + M_CV, cmp_w1_v, 0, 16, 0, P)
                for q in range(2, 12):
                    load_halves(l, S + 13 + q, w_in, 512 * (q % 2), 4, M_G + 512 * (q // 2), 512)
                for m, w, r0 in ((25, w_branch_b, 0), (26, w_branch_c, 0), (27, w_branch_c, 256),
                                 (28, w_branch_a, 0), (29, w_out, 0), (30, w_out, 256), (31, w_out, 512),
                                 (32, w_out, 768)):
                    load_halves(l, S + m, w, r0, 2, 0, D)

            with sp.Fori(0, DEPTH) as l:
                ffn(l, 0, ffn1_w_gate, ffn1_w_up, ffn1_w_down)
                mixer(l)
                ffn(l, 1, ffn2_w_gate, ffn2_w_up, ffn2_w_down)
            v = slab(0, 4)(512)
            sp.wait_ge(lo_done, DEPTH * LAYER_SPLITS - 3 + 1 + 3)
            for part, w in ((v[:, :, 0:FSTEP], ffn1_w_gate), (v[:, :, FSTEP:], ffn1_w_up)):
                sp.dma_start(part, w[0, 0:512, 0:FSTEP].rearrange("(k p) c -> p k c", p=P)).then_inc(raw_in[0], 16)
            sp.wait_ge(x_new, 3 * DEPTH * 4 + 1)
            sp.dma_start(gr[:, 0:D], final_norm.rearrange("(a d) -> a d", a=1).broadcast_to([P, D]))\
                .then_inc(setup_w, 16)
            for t in range(NT):
                sp.wait_ge(x_new, 3 * DEPTH * 4 + 4 + t + 1)
                sp.dma_start(out[0, t * P:(t + 1) * P, :], x[:, t, :]).then_inc(out_done, 16)
            sp.wait_ge(out_done, NT * 16)


_INS = ["x", "ffn1_w_gate", "ffn1_w_up", "ffn1_w_down", "w_in", "cmp_w1_k", "cmp_w2_k", "cmp_w1_v", "cmp_w2_v",
        "w_branch_a", "w_branch_b", "w_branch_c", "w_out", "ffn2_w_gate", "ffn2_w_up", "ffn2_w_down", "final_norm"]
_ROWS = ["ffn1_norm", "mix_norm", "ffn2_norm", "cmp_pos_k", "cmp_pos_v"]


def rope_tables():
    half = HD // 2
    inv = np.float32(10000.0) ** (-np.arange(half, dtype=np.float32) / np.float32(half))
    ang = np.arange(SEQ, dtype=np.float32)[:, None] * inv[None, :].astype(np.float32)
    c, s = np.cos(ang).astype(np.float32), np.sin(ang).astype(np.float32)
    return np.concatenate([c, c], 1), np.concatenate([-s, s], 1)


def kernel(**inputs):
    import concourse.bacc as _bacc
    from concourse.bass_utils import run_bass_kernel_spmd as _run

    nc = _bacc.Bacc("TRN2", target_bir_lowering=False, num_devices=1)
    arrays, args = {}, []
    given = [(name, np.ascontiguousarray(inputs[name])) for name in _INS]
    given.append(("rows", np.concatenate([np.asarray(inputs[name]).reshape(-1, P) for name in _ROWS])))
    given += list(zip(("cos_t", "sin_t"), rope_tables()))
    for name, a in given:
        arrays[f"in_{name}_dram"] = a
        args.append(nc.dram_tensor(f"in_{name}_dram", a.shape, mybir.dt.from_np(a.dtype), kind="ExternalInput").ap())
    args.append(nc.dram_tensor("out_0_dram", (1, SEQ, D), F32, kind="ExternalOutput").ap())
    build(nc, *args)
    r = _run(nc, [arrays], core_ids=[0])
    return r.results[0]["out_0_dram"]
```
